# Optimizing a Trainium2 kernel written in Bass

```python
import math
import jax, jax.numpy as jnp
from jax import lax
import numpy as np

D_MODEL = 1024
BATCH = 1
SEQ = 512
DEPTH = 2

HEAD_DIM = 64
N_HEADS = D_MODEL // HEAD_DIM
MOBA_HEADS = N_HEADS // 4
DIL_HEADS = N_HEADS - MOBA_HEADS
SB_HEAD_DIM = 128
SB_HEADS = D_MODEL // SB_HEAD_DIM
MOBA_BLOCK = 256
MOBA_TOPK = 3
DILATED_PAIRS = ((128, 1), (512, 4), (2048, 16))
Q_BLOCK = 128
SB_GROUP_BLOCKS = 8
SB_CUM = 64
FFN_DIM = ((8 * D_MODEL // 3 + 127) // 128) * 128
CONV_WIDTH = 3
ROPE_THETA = 10000.0
LN_EPS = 1e-5
N_EVEN = (DEPTH + 1) // 2
N_ODD = DEPTH // 2
DEEPNORM_ALPHA = (2 * DEPTH) ** 0.25
DEEPNORM_BETA = (8 * DEPTH) ** -0.25

kernel_name = "hybrid_moba_dilated_stickbreak_convffn"

def layer_norm(x, g, b):
    xf = x.astype(jnp.float32)
    mu = jnp.mean(xf, axis=-1, keepdims=True)
    var = jnp.mean(jnp.square(xf - mu), axis=-1, keepdims=True)
    y = (xf - mu) * lax.rsqrt(var + LN_EPS) * g.astype(jnp.float32) + b.astype(jnp.float32)
    return y.astype(x.dtype)

def rope_tables(S):
    inv = 1.0 / (ROPE_THETA ** (jnp.arange(0, HEAD_DIM, 2, dtype=jnp.float32) / HEAD_DIM))
    ang = jnp.arange(S, dtype=jnp.float32)[:, None] * inv[None, :]
    return jnp.cos(ang), jnp.sin(ang)

def apply_rope(x, cos, sin):
    half = HEAD_DIM // 2
    c = cos.astype(x.dtype)
    s = sin.astype(x.dtype)
    x1, x2 = x[..., :half], x[..., half:]
    return jnp.concatenate([x1 * c - x2 * s, x2 * c + x1 * s], axis=-1)

def split_heads(h, w_qkv, n_heads, head_dim):
    B, S, _ = h.shape
    qkv = (h @ w_qkv).reshape(B, S, 3, n_heads, head_dim)
    qkv = qkv.transpose(2, 0, 3, 1, 4)
    return qkv[0], qkv[1], qkv[2]

def merge_heads(o):
    B, H, S, dh = o.shape
    return o.transpose(0, 2, 1, 3).reshape(B, S, H * dh)

def pad_seq(a, Sp):
    S = a.shape[2]
    return jnp.pad(a, ((0, 0), (0, 0), (0, Sp - S), (0, 0)))

def moba_attention(q, k, v):
    B, H, S, dh = q.shape
    Sp = -(-S // MOBA_BLOCK) * MOBA_BLOCK
    q, k, v = pad_seq(q, Sp), pad_seq(k, Sp), pad_seq(v, Sp)
    NB = Sp // MOBA_BLOCK
    kb = k.reshape(B, H, NB, MOBA_BLOCK, dh)
    vb = v.reshape(B, H, NB, MOBA_BLOCK, dh)
    k_sel_count = min(MOBA_TOPK, NB - 1)
    qblk_all = jnp.arange(Sp) // MOBA_BLOCK
    if k_sel_count > 0:
        kmean = jnp.mean(kb.astype(jnp.float32), axis=3).astype(k.dtype)
        gate = jnp.einsum('bhsd,bhnd->bhsn', q, kmean).astype(jnp.float32)
        past = jnp.arange(NB)[None, :] < qblk_all[:, None]
        gate = jnp.where(past, gate, -jnp.inf)
        _, sel = lax.top_k(gate, k_sel_count)
    bi = jnp.arange(B)[:, None, None, None]
    hi = jnp.arange(H)[None, :, None, None]

    def block(c):
        start = c * Q_BLOCK
        qc = lax.dynamic_slice_in_dim(q, start, Q_BLOCK, axis=2)
        pos = start + jnp.arange(Q_BLOCK)
        own = start // MOBA_BLOCK
        k_own = lax.dynamic_index_in_dim(kb, own, axis=2, keepdims=False)
        v_own = lax.dynamic_index_in_dim(vb, own, axis=2, keepdims=False)
        kpos = own * MOBA_BLOCK + jnp.arange(MOBA_BLOCK)
        s_own = jnp.einsum('bhqd,bhkd->bhqk', qc, k_own).astype(jnp.float32)
        s_own = jnp.where(kpos[None, :] <= pos[:, None], s_own, -jnp.inf)
        if k_sel_count == 0:
            p = jax.nn.softmax(s_own, axis=-1)
            return jnp.einsum('bhqk,bhkd->bhqd', p.astype(v.dtype), v_own).astype(q.dtype)
        idx = lax.dynamic_slice_in_dim(sel, start, Q_BLOCK, axis=2)
        k_g = kb[bi, hi, idx]
        v_g = vb[bi, hi, idx]
        s_sel = jnp.einsum('bhqd,bhqnkd->bhqnk', qc, k_g).astype(jnp.float32)
        valid = idx < (pos // MOBA_BLOCK)[None, None, :, None]
        s_sel = jnp.where(valid[..., None], s_sel, -jnp.inf)
        n_sel = k_sel_count * MOBA_BLOCK
        s_all = jnp.concatenate([s_sel.reshape(B, H, Q_BLOCK, n_sel), s_own], axis=-1)
        p = jax.nn.softmax(s_all, axis=-1).astype(v.dtype)
        p_sel = p[..., :n_sel].reshape(B, H, Q_BLOCK, k_sel_count, MOBA_BLOCK)
        o = (jnp.einsum('bhqnk,bhqnkd->bhqd', p_sel, v_g)
             + jnp.einsum('bhqk,bhkd->bhqd', p[..., n_sel:], v_own))
        return o.astype(q.dtype)

    out = lax.map(block, jnp.arange(Sp // Q_BLOCK))
    out = out.transpose(1, 2, 0, 3, 4).reshape(B, H, Sp, dh)
    return out[:, :, :S]

def dilated_branch(q, k, v, window, dil):
    B, H, S, dh = q.shape
    n_back = window // dil
    span = dil * Q_BLOCK
    Sp = -(-S // span) * span
    n_sub = Sp // dil
    nb = n_sub // Q_BLOCK

    def to_sub(a):
        a = pad_seq(a, Sp).reshape(B, H, n_sub, dil, dh).transpose(0, 1, 3, 2, 4)
        return a.reshape(B, H, dil, nb, Q_BLOCK, dh)

    def with_prev(a):
        prev = jnp.pad(a[:, :, :, :-1], ((0, 0), (0, 0), (0, 0), (1, 0), (0, 0), (0, 0)))
        return jnp.concatenate([prev, a], axis=4)

    qs = to_sub(q)
    ks = with_prev(to_sub(k))
    vs = with_prev(to_sub(v))
    s = jnp.einsum('bhrnqd,bhrnkd->bhrnqk', qs, ks).astype(jnp.float32)
    qi = jnp.arange(Q_BLOCK)[:, None]
    kj = jnp.arange(2 * Q_BLOCK)[None, :]
    diff = qi - kj + Q_BLOCK
    nidx = jnp.arange(nb)[:, None, None]
    mask = (diff >= 0) & (diff <= n_back) & ((nidx > 0) | (kj >= Q_BLOCK))
    s = jnp.where(mask, s, -jnp.inf)
    lse = jax.nn.logsumexp(s, axis=-1)
    p = jnp.exp(s - lse[..., None]).astype(v.dtype)
    o = jnp.einsum('bhrnqk,bhrnkd->bhrnqd', p, vs)
    o = o.reshape(B, H, dil, n_sub, dh).transpose(0, 1, 3, 2, 4).reshape(B, H, Sp, dh)[:, :, :S]
    lse = lse.reshape(B, H, dil, n_sub).transpose(0, 1, 3, 2).reshape(B, H, Sp)[:, :, :S]
    return o, lse

def dilated_attention(q, k, v):
    outs, lses = [], []
    for window, dil in DILATED_PAIRS:
        o, l = dilated_branch(q, k, v, window, dil)
        outs.append(o)
        lses.append(l)
    w = jax.nn.softmax(jnp.stack(lses, axis=0), axis=0)
    out = jnp.sum(w[..., None] * jnp.stack(outs, axis=0).astype(jnp.float32), axis=0)
    return out.astype(q.dtype)

def stick_breaking_attention(q, k, v):
    B, H, S, dh = q.shape
    Sp = -(-S // Q_BLOCK) * Q_BLOCK
    q, k, v = pad_seq(q, Sp), pad_seq(k, Sp), pad_seq(v, Sp)
    n_blk = Sp // Q_BLOCK
    ar = jnp.arange(SB_CUM)
    upper = (ar[None, :] >= ar[:, None]).astype(jnp.float32)
    outs = []
    for g0 in range(0, n_blk, SB_GROUP_BLOCKS):
        nb = min(SB_GROUP_BLOCKS, n_blk - g0)
        L = (g0 + nb) * Q_BLOCK
        kg, vg = k[:, :, :L], v[:, :, :L]
        qg = q[:, :, g0 * Q_BLOCK:L]
        kpos = jnp.arange(L)

        def block(c, qg=qg, kg=kg, vg=vg, kpos=kpos, g0=g0, L=L):
            qc = lax.dynamic_slice_in_dim(qg, c * Q_BLOCK, Q_BLOCK, axis=2)
            t = (g0 + c) * Q_BLOCK + jnp.arange(Q_BLOCK)
            z = jnp.einsum('bhqd,bhsd->bhqs', qc, kg).astype(jnp.float32)
            z = jnp.where(kpos[None, :] < t[:, None], z, -jnp.inf)
            sp = jnp.maximum(z, 0.0) + jnp.log1p(jnp.exp(-jnp.abs(z)))
            spb = sp.reshape(B, H, Q_BLOCK, L // SB_CUM, SB_CUM)
            r_in = jnp.einsum('bhqnk,jk->bhqnj', spb, upper)
            tot = r_in[..., 0]
            off = lax.cumsum(tot, axis=3, reverse=True) - tot
            r = (r_in + off[..., None]).reshape(B, H, Q_BLOCK, L)
            a = jnp.exp(z - r).astype(vg.dtype)
            return jnp.einsum('bhqs,bhsd->bhqd', a, vg).astype(q.dtype)

        outs.append(lax.map(block, jnp.arange(nb)))
    out = jnp.concatenate(outs, axis=0).transpose(1, 2, 0, 3, 4).reshape(B, H, Sp, dh)
    return out[:, :, :S]

def even_mixer(h, w_qkv, w_o, cos, sin):
    q, k, v = split_heads(h, w_qkv, N_HEADS, HEAD_DIM)
    q = apply_rope(q, cos, sin) * (HEAD_DIM ** -0.5)
    k = apply_rope(k, cos, sin)
    oa = moba_attention(q[:, :MOBA_HEADS], k[:, :MOBA_HEADS], v[:, :MOBA_HEADS])
    ob = dilated_attention(q[:, MOBA_HEADS:], k[:, MOBA_HEADS:], v[:, MOBA_HEADS:])
    o = jnp.concatenate([oa, ob], axis=1)
    return merge_heads(o) @ w_o

def odd_mixer(h, w_qkv, w_o):
    q, k, v = split_heads(h, w_qkv, SB_HEADS, SB_HEAD_DIM)
    o = stick_breaking_attention(q * (SB_HEAD_DIM ** -0.5), k, v)
    return merge_heads(o) @ w_o

def conv_ffn(h, w_up, conv_w, conv_b, w_down):
    S = h.shape[1]
    u = h @ w_up
    up = jnp.pad(u, ((0, 0), (CONV_WIDTH - 1, 0), (0, 0)))
    c = conv_b
    for j in range(CONV_WIDTH):
        c = c + conv_w[j] * up[:, j:j + S]
    g, val = c[..., :FFN_DIM], c[..., FFN_DIM:]
    return (jax.nn.silu(g) * val) @ w_down

def setup_inputs(seed: int = 0) -> dict:
    key = jax.random.key(seed)
    ks = jax.random.split(key, 20)
    D, F = D_MODEL, FFN_DIM
    sd = D ** -0.5

    def qkv_weight(k0, n):
        a, b, c = jax.random.split(k0, 3)
        wq = jax.random.normal(a, (n, D, D), jnp.float32) * sd
        wk = jax.random.normal(b, (n, D, D), jnp.float32) * sd
        wv = jax.random.normal(c, (n, D, D), jnp.float32) * sd * DEEPNORM_BETA
        return jnp.concatenate([wq, wk, wv], axis=-1)

    return {
        "x": jax.random.normal(ks[0], (BATCH, SEQ, D), jnp.float32),
        "w_qkv_ab": qkv_weight(ks[1], N_EVEN),
        "w_o_ab": jax.random.normal(ks[2], (N_EVEN, D, D), jnp.float32) * sd * DEEPNORM_BETA,
        "w_qkv_c": qkv_weight(ks[3], N_ODD),
        "w_o_c": jax.random.normal(ks[4], (N_ODD, D, D), jnp.float32) * sd * DEEPNORM_BETA,
        "ln_mix_g": 1.0 + 0.02 * jax.random.normal(ks[5], (DEPTH, D), jnp.float32),
        "ln_mix_b": 0.02 * jax.random.normal(ks[6], (DEPTH, D), jnp.float32),
        "w_up": jax.random.normal(ks[7], (DEPTH, D, 2 * F), jnp.float32) * sd * DEEPNORM_BETA,
        "conv_w": jax.random.normal(ks[8], (DEPTH, CONV_WIDTH, 2 * F), jnp.float32) * CONV_WIDTH ** -0.5,
        "conv_b": 0.01 * jax.random.normal(ks[9], (DEPTH, 2 * F), jnp.float32),
        "w_down": jax.random.normal(ks[10], (DEPTH, F, D), jnp.float32) * F ** -0.5 * DEEPNORM_BETA,
        "ln_ffn_g": 1.0 + 0.02 * jax.random.normal(ks[11], (DEPTH, D), jnp.float32),
        "ln_ffn_b": 0.02 * jax.random.normal(ks[12], (DEPTH, D), jnp.float32),
    }

def reference(x, w_qkv_ab, w_o_ab, w_qkv_c, w_o_c, ln_mix_g, ln_mix_b,
              w_up, conv_w, conv_b, w_down, ln_ffn_g, ln_ffn_b):
    cos, sin = rope_tables(x.shape[1])
    for i in range(DEPTH):
        if i % 2 == 0:
            m = even_mixer(x, w_qkv_ab[i // 2], w_o_ab[i // 2], cos, sin)
        else:
            m = odd_mixer(x, w_qkv_c[i // 2], w_o_c[i // 2])
        x = layer_norm(DEEPNORM_ALPHA * x + m.astype(x.dtype), ln_mix_g[i], ln_mix_b[i])
        f = conv_ffn(x, w_up[i], conv_w[i], conv_b[i], w_down[i])
        x = layer_norm(DEEPNORM_ALPHA * x + f.astype(x.dtype), ln_ffn_g[i], ln_ffn_b[i])
    return x


_drawn_inputs = setup_inputs


def setup_inputs(seed=0):
    import zlib

    import numpy as np

    out = dict(_drawn_inputs(seed))
    spreads = {}
    factors = {'conv_b': 29.443}
    for name, (base, spread) in spreads.items():
        noise = np.random.default_rng([zlib.crc32(name.encode()), seed]).standard_normal(out[name].shape)
        drawn = base * np.exp(spread * noise) if base else spread * noise
        out[name] = __import__('jax').numpy.asarray(drawn.astype(out[name].dtype))
    for name, factor in factors.items():
        out[name] = (out[name] * factor).astype(out[name].dtype)
    return out
```

```python
from contextlib import ExitStack

import concourse.bass as bass
from concourse import mybir

F32 = mybir.dt.float32
F32R = mybir.dt.float32r
ACT = mybir.ActivationFunctionType
ALU = mybir.AluOpType

P = 128
S, D, DEPTH = 512, 1024, 2
F = ((8 * D // 3 + 127) // 128) * 128
KD = D // P
KF = F // P
NT = S // P
HALF = D // 2
NPOS = 8
ALPHA = (2 * DEPTH) ** 0.25
EPS = 1e-5
SB_SCALE = 128 ** -0.5
MOBA_SCALE = 64 ** -0.5
FORBID = 1e30
UNIT = D

N_V, N_QK, N_O, N_UP, N_DN = KD // 2, NPOS, KD // 2, KF, KF // 2
AT_QK = N_V
AT_O = AT_QK + N_QK
AT_UP = AT_O + N_O
AT_DN = AT_UP + N_UP
PER_LAYER = AT_DN + N_DN
STEPS = DEPTH * PER_LAYER


def build(nc, x_in, w_stream, ident_in, rope_in, mask_in, tri_in, conv_in, ln_in, out):
    ctx = ExitStack()
    with ctx:
        def sb(name, shape, dt=F32, stack=ctx):
            return stack.enter_context(nc.sbuf_tensor(name, shape, dt))

        def sem(name):
            return ctx.enter_context(nc.semaphore(name))

        bank = [ctx.enter_context(nc.psum_tensor(f"bank{b}", [P, 512], F32)) for b in range(8)]

        w_raw = [sb(f"w_raw{s}", [P, 2 * UNIT]) for s in range(2)]
        w_hi = [sb(f"w_hi{s}", [P, 2 * UNIT], F32R) for s in range(2)]
        w_lo = [sb(f"w_lo{s}", [P, 2 * UNIT], F32R) for s in range(2)]
        xt_hi = sb("xt_hi", [P, KD, S], F32R)
        xt_lo = sb("xt_lo", [P, KD, S], F32R)
        a_hi = sb("a_hi", [P, KD, S], F32R)
        a_lo = sb("a_lo", [P, KD, S], F32R)
        x = sb("x", [P, NT, D])
        gain = sb("gain", [P, D])
        shift = sb("shift", [P, D])
        ident = sb("ident", [P, P])
        conv = sb("conv", [P, DEPTH * 2 * KF * 4])
        eps = sb("eps", [P, 1])
        stat = sb("stat", [P, NT, 10])

        with ExitStack() as st:
            v_all = sb("v_all", [P, NT, D], stack=st)
            v_pos = [sb(f"v_pos{s}", [P, NT, P], stack=st) for s in range(2)]
            probs_t = [sb(f"probs_t{h}", [P, NT, S], stack=st) for h in range(2)]
            qa = [sb(f"qa{s}", [P, 2, S], stack=st) for s in range(2)]
            ka = [sb(f"ka{s}", [P, S], stack=st) for s in range(2)]
            probs = [sb(f"probs{s}", [P, S], stack=st) for s in range(2)]
            with ExitStack() as ev:
                rope = sb("rope", [P, 2, S], stack=ev)
                masks = sb("masks", [P, 2, S], stack=ev)
                qc = sb("qc", [P, S], stack=ev)
                qs = sb("qs", [P, S], stack=ev)
                kc = sb("kc", [P, S], stack=ev)
                ks = sb("ks", [P, S], stack=ev)
                sm = sb("sm", [P, 2, 4], stack=ev)
            with ExitStack() as od:
                soft = [sb(f"soft{s}", [P, S], stack=od) for s in range(2)]
                tri = sb("tri", [P, P], stack=od)
        with ExitStack() as st:
            h_all = sb("h_all", [P, KF, S], stack=st)
            cg = [sb(f"cg{s}", [P, S], stack=st) for s in range(2)]
            cv = [sb(f"cv{s}", [P, S], stack=st) for s in range(2)]
            sig = [sb(f"sig{s}", [P, S], stack=st) for s in range(2)]
        with ExitStack() as st:
            sb("below_ln", [P, KF, S], stack=st)
            ln_mul = sb("ln_mul", [P, D], stack=st)
            ln_junk = sb("ln_junk", [P, D], stack=st)

        raw_full = [sem(f"raw_full{s}") for s in range(2)]
        hi_ready = sem("hi_ready")
        lo_ready = sem("lo_ready")
        w_used = sem("w_used")
        x_full = [sem(f"x_full{t}") for t in range(NT)]
        const_full = sem("const_full")
        even_full = sem("even_full")
        tri_full = sem("tri_full")
        gb_full = sem("gb_full")
        set_ready = sem("set_ready")
        out_done = sem("out_done")

        def tap(l, tile, k):
            return conv[:, bass.ds((tile + l * 2 * KF) * 4 + k, 1)]

        class Phase:
            def __init__(self, tag, names):
                self.by = {n: sem(f"{tag}_{n}") for n in names.split()}

            def __getitem__(self, n):
                return self.by[n]

        V = [Phase(f"v{l}", "rows act dve") for l in range(DEPTH)]
        A = [Phase(f"a{l}", "q_mm q_cp k_cp q_sw k_sw q_m k_m q_ok k_ok s_mm s_rd ex rc p_ok t_mm "
                            "tev_a tev_v v_pos pv ot_hi ot_lo zm ab e1 ln sp sc rr") for l in range(DEPTH)]
        N = [Phase(f"n{i}", "rows sum mean sq lv y0 va nt mulg xn") for i in range(2 * DEPTH)]
        T = [Phase(f"t{i}", "mm hi lo") for i in range(2 * DEPTH)]
        U = [Phase(f"u{l}", "g_mm cg cv g1 gc sg m1 v1 vc h") for l in range(DEPTH)]
        DN = [Phase(f"d{l}", "a_hi a_lo") for l in range(DEPTH)]

        block = ctx.enter_context(nc.Block())

        def filled(c, it):
            return 16 * (c // 2 + it + 1)

        @block.sync
        def _(sp):
            for t in range(NT):
                sp.dma_start(x[:, t, :], x_in[t * P:(t + 1) * P, :]).then_inc(x_full[t], 16)
                if t == 0:
                    for s in range(2):
                        sp.dma_start(w_raw[s][:, :], w_stream[s]).then_inc(raw_full[s], 16)
            with sp.Fori(1, STEPS // 2) as it:
                for s in range(2):
                    sp.wait_ge(lo_ready, 4 * it + 2 * s - 2)
                    sp.dma_start(w_raw[s][:, :], w_stream[2 * it + s]).then_inc(raw_full[s], 16)
            for t in range(NT):
                sp.wait_ge(N[-1]["xn"], t + 1)
                sp.dma_start(out[t * P:(t + 1) * P, :], x[:, t, :]).then_inc(out_done, 16)
            sp.wait_ge(out_done, 16 * NT)

        @block.gpsimd
        def _(pool):
            def rest(c, it=0):
                pool.wait_ge(hi_ready, c + 2 * it + 1)
                s = c % 2
                for u in range(2):
                    part = slice(u * UNIT, (u + 1) * UNIT)
                    pool.tensor_tensor(w_lo[s][:, part], w_raw[s][:, part],
                                       w_hi[s][:, part].bitcast(F32), ALU.subtract).then_inc(lo_ready, 1)

            rest(0)
            for l in range(DEPTH):
                b = l * PER_LAYER
                for c in range(1, AT_QK + 1):
                    rest(b + c)
                for sname in ("act", "dve"):
                    pool.wait_ge(V[l][sname], NT)
                with pool.Fori(0, NPOS // 2) as it:
                    for j in range(2):
                        rest(b + AT_QK + 1 + j, it)
                        pool.wait_ge(w_used, b + AT_QK + 2 * it + j + 1)
                        pool.tensor_copy(v_pos[j][:, :, :], v_all[:, :, bass.ds((2 * it + j) * P, P)])\
                            .then_inc(A[l]["v_pos"], 1)
                first = b + AT_O + 1
                n = min(b + PER_LAYER + 1, STEPS) - first
                with pool.Fori(0, n // 2) as it:
                    for j in range(2):
                        rest(first + j, it)
                if n % 2:
                    rest(first + n - 1)

        @block.scalar
        def _(act):
            def heads(c, it=0, used=True):
                act.wait_ge(raw_full[c % 2], filled(c, it))
                if used:
                    act.wait_ge(w_used, c + 2 * it - 1)
                act.activation(w_hi[c % 2][:, :], w_raw[c % 2][:, :], ACT.Copy).then_inc(hi_ready, 1)

            def load_gain(i):
                for row, dst in ((0, gain), (1, shift)):
                    act.dma_start(dst[:, :], ln_in[i, row:row + 1, :].broadcast_to([P, D])).then_inc(gb_full, 16)

            def xt_heads(i, t):
                act.wait_ge(T[i]["mm"], t + 1)
                for g in range(2):
                    act.activation(xt_hi[:, 4 * g:4 * g + 4, t * P:(t + 1) * P],
                                   bank[2 * t + g][:, :].rearrange("p (k q) -> p k q", k=4),
                                   ACT.Copy).then_inc(T[i]["hi"], 1)

            def norm_stats(i, t):
                n = N[i]
                act.wait_ge(n["mean"], t + 1)
                act.activation(ln_junk[:, :], x[:, t, :], ACT.Square, bias=stat[:, t, 2:3],
                               accum_out=stat[:, t, 3:4]).then_inc(n["sq"], 1)
                act.wait_ge(n["sq"], t + 1)
                act.activation(stat[:, t, 4:5], stat[:, t, 3:4], ACT.Ln, bias=eps[:, 0:1],
                               scale=1.0 / D).then_inc(n["lv"], 1)
                act.wait_ge(n["lv"], t + 1)
                act.activation(stat[:, t, 5:6], stat[:, t, 4:5], ACT.Exp, scale=-0.5).then_inc(n["y0"], 1)

            def values(l):
                for t in range(NT):
                    if t < NT - 1:
                        act.wait_ge(V[l]["rows"], t + 1)
                    else:
                        act.wait_ge(w_used, l * PER_LAYER + AT_QK)
                    act.activation(v_all[:, t, 0:HALF], bank[2 * t][:, :], ACT.Copy).then_inc(V[l]["act"], 1)

            def swap(dst, src, signal):
                for a in range(4):
                    o = (a ^ 1) * 32
                    act.dma_start(dst[32 * a:32 * a + 32, :], src[o:o + 32, :]).then_inc(signal, 16)

            def turn_out(a, j, steps, g):
                act.wait_ge(a["t_mm"], g + 1)
                qi = j % NT
                act.activation(probs_t[j // NT][:, 0:qi + 1, qi * P:(qi + 1) * P],
                               bank[4 + j % 2][:, 0:(qi + 1) * P].rearrange("p (k q) -> p k q", q=P),
                               ACT.Copy).then_inc(a["tev_a"], 1)

            def out_heads(a, i, slot):
                act.wait_ge(a["pv"], i + 1)
                act.activation(a_hi[:, bass.ds(i, 1), :],
                               bank[6 + slot][:, :].rearrange("p (a q) -> p a q", a=1),
                               ACT.Copy).then_inc(a["ot_hi"], 1)

            def even_body(b, c, it, dense):
                a = A[0]
                i = c + 2 * it
                heads(b + AT_QK + c + 2, it)
                for j in range(8):
                    g = 8 * i + j
                    if j % 2 == 1 and j >= 3:
                        turn_out(a, j - 2, 8, g - 2)
                    if j == 4 and dense:
                        act.wait_ge(a["q_mm"], i + 2)
                        act.activation(qc[:, :], bank[0][:, :], ACT.Copy, scale=-MOBA_SCALE).then_inc(a["q_cp"], 1)
                        act.wait_ge(a["q_cp"], i + 2)
                        swap(qs, qc, a["q_sw"])
                    if j == 7 and dense:
                        act.wait_ge(w_used, b + AT_QK + i + 2)
                        act.activation(kc[:, :], bank[1][:, :], ACT.Copy).then_inc(a["k_cp"], 1)
                        act.wait_ge(a["k_cp"], i + 2)
                        swap(ks, kc, a["k_sw"])
                    act.wait_ge(a["s_rd"], g + 1)
                    L = (j % NT + 1) * P
                    act.activation(probs[j % 2][:, 0:L], probs[j % 2][:, 0:L], ACT.Exp,
                                   bias=sm[:, j % 2, 0:1], scale=-1.0,
                                   accum_out=sm[:, j % 2, 1:2]).then_inc(a["ex"], 1)
                turn_out(a, 7, 8, 8 * i + 7)
                out_heads(a, i, c % 2)

            def odd_body(b, c, it, dense):
                a = A[1]
                i = c + 2 * it
                heads(b + AT_QK + c + 2, it)

                def soft_part(j):
                    g, L = 4 * i + j, (j + 1) * P
                    e = soft[j % 2][:, 0:L]
                    act.wait_ge(a["zm"], g + 1)
                    act.activation(e, bank[2 + j % 2][:, 0:L], ACT.Abs).then_inc(a["ab"], 1)
                    act.wait_ge(a["ab"], g + 1)
                    act.activation(e, e, ACT.Exp, scale=-1.0).then_inc(a["e1"], 1)
                    act.wait_ge(a["e1"], g + 1)
                    act.activation(e, e, ACT.Ln, bias=1.0).then_inc(a["ln"], 1)

                def weight_part(j):
                    g, L = 4 * i + j, (j + 1) * P
                    act.wait_ge(a["rr"], g + 1)
                    act.activation(probs[j % 2][:, 0:L], probs[j % 2][:, 0:L], ACT.Exp).then_inc(a["p_ok"], 1)

                for j in range(4):
                    if j == 3:
                        turn_out(a, 1, 4, 4 * i + 1)
                        if dense:
                            act.wait_ge(a["q_mm"], i + 2)
                            act.activation(qa[(c + 1) % 2][:, 0, :], bank[0][:, :], ACT.Copy,
                                           scale=SB_SCALE).then_inc(a["q_ok"], 1)
                    soft_part(j)
                    if j >= 1:
                        weight_part(j - 1)
                weight_part(3)
                if dense:
                    act.wait_ge(w_used, b + AT_QK + i + 2)
                    act.activation(ka[(c + 1) % 2][:, :], bank[1][:, :], ACT.Copy).then_inc(a["k_ok"], 1)
                turn_out(a, 3, 4, 4 * i + 3)
                out_heads(a, i, c % 2)

            act.dma_start(ident[:, :], ident_in).then_inc(const_full, 16)
            act.dma_start(conv[:, :], conv_in).then_inc(const_full, 16)
            act.dma_start(rope[:, :, :], rope_in).then_inc(even_full, 16)
            act.dma_start(masks[:, :, :], mask_in).then_inc(even_full, 16)
            load_gain(0)
            heads(0, used=False)
            heads(1, used=False)
            act.wait_ge(set_ready, 5)
            for t in range(NT):
                xt_heads(0, t)

            for l in range(DEPTH):
                b = l * PER_LAYER
                for c in range(3):
                    heads(b + 2 + c)
                values(l)
                heads(b + 5)
                if l == 0:
                    a = A[0]
                    act.wait_ge(a["q_mm"], 1)
                    act.activation(qc[:, :], bank[0][:, :], ACT.Copy, scale=-MOBA_SCALE).then_inc(a["q_cp"], 1)
                    act.wait_ge(a["q_cp"], 1)
                    swap(qs, qc, a["q_sw"])
                    act.wait_ge(w_used, b + AT_QK + 1)
                    act.activation(kc[:, :], bank[1][:, :], ACT.Copy).then_inc(a["k_cp"], 1)
                    act.wait_ge(a["k_cp"], 1)
                    swap(ks, kc, a["k_sw"])
                    body = even_body
                else:
                    a = A[1]
                    act.wait_ge(N[1]["xn"], NT)
                    act.dma_start(tri[:, :], tri_in).then_inc(tri_full, 16)
                    act.wait_ge(a["q_mm"], 1)
                    act.activation(qa[0][:, 0, :], bank[0][:, :], ACT.Copy, scale=SB_SCALE).then_inc(a["q_ok"], 1)
                    act.wait_ge(w_used, b + AT_QK + 1)
                    act.activation(ka[0][:, :], bank[1][:, :], ACT.Copy).then_inc(a["k_ok"], 1)
                    body = odd_body
                with act.Fori(0, 3) as it:
                    body(b, 0, it, True)
                    body(b, 1, it, True)
                body(b, 6, 0, True)
                body(b, 7, 0, False)
                for c in range(2):
                    heads(b + AT_O + 2 + c)
                for i, after in ((2 * l, b + AT_O + 4), (2 * l + 1, b + PER_LAYER)):
                    if i % 2:
                        def up_body(c, it, first):
                            f, u = c + 2 * it, U[l]
                            s = c % 2
                            act.wait_ge(u["g_mm"], f + 1)
                            if not first:
                                act.wait_ge(u["h"], f - 1)
                            act.activation(cg[s][:, :], bank[2 * s][:, :], ACT.Identity,
                                           bias=tap(l, f, 3),
                                           scale=tap(l, f, 2)).then_inc(u["cg"], 1)
                            heads(b + AT_UP + c + 2, it)
                            act.wait_ge(u["gc"], f + 1)
                            act.activation(sig[s][:, :], cg[s][:, :], ACT.Sigmoid).then_inc(u["sg"], 1)
                            act.wait_ge(w_used, b + AT_UP + f + 1)
                            act.activation(cv[s][:, :], bank[2 * s + 1][:, :], ACT.Identity,
                                           bias=tap(l, f + KF, 3),
                                           scale=tap(l, f + KF, 2)).then_inc(u["cv"], 1)

                        up_body(0, 0, True)
                        up_body(1, 0, True)
                        with act.Fori(1, KF // 2) as it:
                            up_body(0, it, False)
                            up_body(1, it, False)

                        def chunk_heads(c, it=0):
                            j = c + 2 * it
                            act.wait_ge(U[l]["h"], 2 * j + 2)
                            act.wait_ge(w_used, b + AT_DN + j - 1)
                            act.activation(a_hi[:, 2 * (c % 2):2 * (c % 2) + 2, :],
                                           h_all[:, bass.ds(2 * j, 2), :], ACT.Copy).then_inc(DN[l]["a_hi"], 1)

                        chunk_heads(0)
                        chunk_heads(1)
                        chunk_heads(2)
                        heads(b + AT_DN + 2)
                        with act.Fori(0, 4) as it:
                            for j in (1, 2):
                                chunk_heads(j + 2, it)
                                heads(b + AT_DN + 2 + j, it)
                    for t in range(NT):
                        norm_stats(i, t)
                        if i < 2 * DEPTH - 1:
                            if t == NT - 1:
                                heads(after)
                            xt_heads(i + 1, t)
                    if i < 2 * DEPTH - 1:
                        heads(after + 1)
                        act.wait_ge(N[i]["xn"], NT)
                        load_gain(i + 1)

        @block.vector
        def _(dve):
            def xt_rests(i, t):
                dve.wait_ge(T[i]["hi"], 2 * t + 2)
                for g in range(2):
                    part = xt_hi[:, 4 * g:4 * g + 4, t * P:(t + 1) * P]
                    dve.tensor_tensor(xt_lo[:, 4 * g:4 * g + 4, t * P:(t + 1) * P],
                                      bank[2 * t + g][:, :].rearrange("p (k q) -> p k q", k=4),
                                      part.bitcast(F32), ALU.subtract).then_inc(T[i]["lo"], 1)

            def norm_a(i, t):
                n = N[i]
                if t < NT - 1:
                    dve.wait_ge(n["rows"], t + 1)
                else:
                    dve.wait_ge(w_used, i // 2 * PER_LAYER + (PER_LAYER if i % 2 else AT_UP))
                for g in range(2):
                    dve.scalar_tensor_tensor(out=x[:, t, g * HALF:(g + 1) * HALF],
                                             in0=x[:, t, g * HALF:(g + 1) * HALF], scalar=ALPHA,
                                             in1=bank[2 * t + g][:, :], op0=ALU.mult, op1=ALU.add,
                                             accum_out=stat[:, t, g:g + 1]).then_inc(n["sum"], 1)
                dve.wait_ge(n["sum"], 2 * t + 2)
                dve.tensor_scalar(stat[:, t, 2:3], stat[:, t, 0:1], stat[:, t, 1:2], -1.0 / D,
                                  ALU.add, ALU.mult).then_inc(n["mean"], 1)
                dve.wait_ge(n["mean"], t + 1)
                if t == 0:
                    dve.wait_ge(gb_full, 32 * (i + 1))
                else:
                    dve.wait_ge(n["xn"], t)
                dve.scalar_tensor_tensor(out=ln_mul[:, :], in0=x[:, t, :], scalar=stat[:, t, 2:3],
                                         in1=gain[:, :], op0=ALU.add, op1=ALU.mult).then_inc(n["mulg"], 1)

            def norm_b(i, t):
                n = N[i]
                v, y0, w, r = (stat[:, t, k:k + 1] for k in (6, 5, 7, 8))
                dve.wait_ge(n["sq"], t + 1)
                dve.tensor_scalar(v, stat[:, t, 3:4], 1.0 / D, EPS, ALU.mult, ALU.add).then_inc(n["va"], 1)
                dve.wait_ge(n["va"], t + 1)
                dve.wait_ge(n["y0"], t + 1)
                dve.scalar_tensor_tensor(out=w, in0=y0, scalar=v, in1=y0, op0=ALU.mult,
                                         op1=ALU.mult).then_inc(n["nt"], 1)
                dve.wait_ge(n["nt"], 3 * t + 1)
                dve.tensor_scalar(w, w, -0.5, 1.5, ALU.mult, ALU.add).then_inc(n["nt"], 1)
                dve.wait_ge(n["nt"], 3 * t + 2)
                dve.tensor_tensor(r, y0, w, ALU.mult).then_inc(n["nt"], 1)
                dve.wait_ge(n["nt"], 3 * t + 3)
                dve.wait_ge(n["mulg"], t + 1)
                dve.scalar_tensor_tensor(out=x[:, t, :], in0=ln_mul[:, :], scalar=r, in1=shift[:, :],
                                         op0=ALU.mult, op1=ALU.add).then_inc(n["xn"], 1)

            def norm(i):
                for t in range(NT):
                    norm_a(i, t)
                    if t >= 1 and i < 2 * DEPTH - 1:
                        xt_rests(i + 1, t - 1)
                    norm_b(i, t)
                if i < 2 * DEPTH - 1:
                    xt_rests(i + 1, NT - 1)

            def rope_mul(t, tab, ready, count, done):
                dve.wait_ge(ready, count)
                dve.tensor_tensor(t[:, :], t[:, :], rope[:, tab, :], ALU.mult).then_inc(done, 1)

            def rope_q(a, s, i):
                dve.wait_ge(a["q_m"], 2 * i + 2)
                for h in range(2):
                    part = slice(64 * h, 64 * h + 64)
                    dve.tensor_tensor(qa[s][part, h, :], qc[part, :], qs[part, :], ALU.add).then_inc(a["q_ok"], 1)

            def rope_k(a, s, i):
                rope_mul(kc, 0, a["k_sw"], 64 * (i + 1), a["k_m"])
                rope_mul(ks, 1, a["k_sw"], 64 * (i + 1), a["k_m"])
                dve.wait_ge(a["k_m"], 2 * i + 2)
                dve.tensor_tensor(ka[s][:, :], kc[:, :], ks[:, :], ALU.add).then_inc(a["k_ok"], 1)

            def turn_out(a, j, g):
                dve.wait_ge(a["t_mm"], g + 1)
                qi = j % NT
                dve.tensor_copy(probs_t[j // NT][:, 0:qi + 1, qi * P:(qi + 1) * P],
                                bank[4 + j % 2][:, 0:(qi + 1) * P].rearrange("p (k q) -> p k q", q=P))\
                    .then_inc(a["tev_v"], 1)

            def out_rests(a, i, par):
                dve.wait_ge(a["ot_hi"], i + 1)
                dve.tensor_tensor(a_lo[:, bass.ds(i, 1), :],
                                  bank[6 + par][:, :].rearrange("p (a q) -> p a q", a=1),
                                  a_hi[:, bass.ds(i, 1), :].bitcast(F32), ALU.subtract).then_inc(a["ot_lo"], 1)

            def even_body(c, it, dense, kind):
                a, i = A[0], c + 2 * it

                def bound(j):
                    g, qi = 8 * i + j, j % NT
                    L = (qi + 1) * P
                    dve.wait_ge(a["s_mm"], g + 1)
                    dve.memset(sm[:, j % 2, 3:4], 0.0)
                    dve.tensor_tensor_reduce(probs[j % 2][:, 0:L], bank[2 + j % 2][:, 0:L],
                                             masks[:, kind, S - L:S], 1.0, 3e38, ALU.add, ALU.min,
                                             sm[:, j % 2, 0:1]).then_inc(a["s_rd"], 1)

                def divide(j):
                    g, L = 8 * i + j, (j % NT + 1) * P
                    dve.wait_ge(a["ex"], g + 1)
                    dve.reciprocal(sm[:, j % 2, 2:3], sm[:, j % 2, 1:2]).then_inc(a["rc"], 1)
                    dve.wait_ge(a["rc"], g + 1)
                    dve.tensor_scalar(probs[j % 2][:, 0:L], probs[j % 2][:, 0:L], sm[:, j % 2, 2:3], None,
                                      ALU.mult).then_inc(a["p_ok"], 1)

                for j in range(8):
                    if j >= 2 and j % 2 == 0:
                        turn_out(a, j - 2, 8 * i + j - 2)
                    bound(j)
                    if j >= 1:
                        divide(j - 1)
                    if dense and j == 5:
                        rope_mul(qc, 0, a["q_sw"], 64 * (i + 2), a["q_m"])
                    if dense and j == 6:
                        rope_mul(qs, 1, a["q_sw"], 64 * (i + 2), a["q_m"])
                divide(7)
                turn_out(a, 6, 8 * i + 6)
                if dense:
                    rope_q(a, (c + 1) % 2, i + 1)
                    rope_k(a, (c + 1) % 2, i + 1)
                out_rests(a, i, c % 2)

            def odd_body(c, it, dense, kind):
                a, i = A[1], c + 2 * it

                def mask_diagonal(j):
                    dve.wait_ge(a["s_mm"], 4 * i + j + 1)
                    z = bank[2 + j % 2][:, j * P:(j + 1) * P]
                    dve.tensor_tensor(z, z, tri[:, :], ALU.add).then_inc(a["zm"], 1)

                def break_stick(j):
                    g, L = 4 * i + j, (j + 1) * P
                    z, e, r = bank[2 + j % 2][:, 0:L], soft[j % 2], probs[j % 2]
                    dve.wait_ge(a["ln"], g + 1)
                    dve.scalar_tensor_tensor(out=e[:, 0:L], in0=z, scalar=0.0, in1=e[:, 0:L],
                                             op0=ALU.max, op1=ALU.add).then_inc(a["sp"], 1)
                    dve.wait_ge(a["sp"], g + 1)
                    back = e[:, L - 1::-1]
                    dve.tensor_tensor_scan(r[:, L - 1::-1], back, back, 0.0, ALU.add,
                                           ALU.max).then_inc(a["sc"], 1)
                    dve.wait_ge(a["sc"], g + 1)
                    dve.tensor_tensor(r[:, 0:L], z, r[:, 0:L], ALU.subtract).then_inc(a["rr"], 1)

                for j in range(4):
                    if j == 2:
                        turn_out(a, 0, 4 * i)
                    mask_diagonal(j)
                    if j >= 1:
                        break_stick(j - 1)
                break_stick(3)
                turn_out(a, 2, 4 * i + 2)
                out_rests(a, i, c % 2)

            dve.memset(eps[:, :], EPS).then_inc(set_ready, 1)
            for s in range(2):
                dve.memset(qa[s][P // 2:P, 0, :], 0.0).then_inc(set_ready, 1)
                dve.memset(qa[s][0:P // 2, 1, :], 0.0).then_inc(set_ready, 1)
            dve.wait_ge(set_ready, 5)
            for t in range(NT):
                xt_rests(0, t)
            for l in range(DEPTH):
                for t in range(NT):
                    if t < NT - 1:
                        dve.wait_ge(V[l]["rows"], t + 1)
                    else:
                        dve.wait_ge(w_used, l * PER_LAYER + AT_QK)
                    dve.tensor_copy(v_all[:, t, HALF:D], bank[2 * t + 1][:, :]).then_inc(V[l]["dve"], 1)
                if l == 0:
                    a = A[0]
                    dve.wait_ge(even_full, 32)
                    rope_mul(qc, 0, a["q_sw"], 64, a["q_m"])
                    rope_mul(qs, 1, a["q_sw"], 64, a["q_m"])
                    rope_q(a, 0, 0)
                    rope_k(a, 0, 0)
                    body = even_body
                else:
                    dve.wait_ge(tri_full, 16)
                    body = odd_body
                with dve.Fori(0, 3) as it:
                    body(0, it, True, 0)
                    body(1, it, True, 0)
                body(6, 0, True, 1)
                body(7, 0, False, 1)
                norm(2 * l)

                def up_body(c, it):
                    f, u, s = c + 2 * it, U[l], c % 2

                    def convolve(ps, acc, tile, start, mid, end):
                        dve.wait_ge(start, f + 1)
                        dve.scalar_tensor_tensor(out=acc[:, 1:S], in0=ps[:, 0:S - 1],
                                                 scalar=tap(l, tile, 1), in1=acc[:, 1:S],
                                                 op0=ALU.mult, op1=ALU.add).then_inc(mid, 1)
                        dve.wait_ge(mid, f + 1)
                        dve.scalar_tensor_tensor(out=acc[:, 2:S], in0=ps[:, 0:S - 2],
                                                 scalar=tap(l, tile, 0), in1=acc[:, 2:S],
                                                 op0=ALU.mult, op1=ALU.add).then_inc(end, 1)

                    convolve(bank[2 * s], cg[s], f, u["cg"], u["g1"], u["gc"])
                    dve.wait_ge(u["sg"], f + 1)
                    dve.tensor_tensor(sig[s][:, :], sig[s][:, :], cg[s][:, :], ALU.mult).then_inc(u["m1"], 1)
                    convolve(bank[2 * s + 1], cv[s], f + KF, u["cv"], u["v1"], u["vc"])
                    dve.wait_ge(u["vc"], f + 1)
                    dve.wait_ge(u["m1"], f + 1)
                    dve.tensor_tensor(h_all[:, bass.ds(f, 1), :],
                                      sig[s][:, :].rearrange("p (a q) -> p a q", a=1),
                                      cv[s][:, :].rearrange("p (a q) -> p a q", a=1), ALU.mult).then_inc(u["h"], 1)

                with dve.Fori(0, KF // 2) as it:
                    up_body(0, it)
                    up_body(1, it)

                def chunk_rests(c, it=0):
                    j = c + 2 * it
                    dve.wait_ge(DN[l]["a_hi"], j + 1)
                    k = 2 * (c % 2)
                    dve.tensor_tensor(a_lo[:, k:k + 2, :], h_all[:, bass.ds(2 * j, 2), :],
                                      a_hi[:, k:k + 2, :].bitcast(F32), ALU.subtract).then_inc(DN[l]["a_lo"], 1)

                chunk_rests(0)
                with dve.Fori(0, N_DN // 2) as it:
                    chunk_rests(1, it)
                    chunk_rests(2, it)
                norm(2 * l + 1)

        @block.tensor
        def _(pe):
            def turn_x(i):
                for t in range(NT):
                    if i == 0:
                        pe.wait_ge(x_full[t], 16)
                    else:
                        pe.wait_ge(N[i - 1]["xn"], t + 1)
                    for k in range(KD):
                        mm = pe.transpose(bank[2 * t + k // 4][:, (k % 4) * P:(k % 4 + 1) * P],
                                          x[:, t, k * P:(k + 1) * P], ident[:, :])
                    mm.then_inc(T[i]["mm"], 1)

            def row_steps(steps, a, first_chunk, last, rows, wait):
                for t in range(NT):
                    wait(t)
                    for c, it, slot in steps:
                        s = c % 2
                        for u in range(2):
                            if t == 0:
                                pe.wait_ge(lo_ready, 2 * (c + 2 * it) + u + 1)
                            hi = a[0][:, slot + u, t * P:(t + 1) * P]
                            lo = a[1][:, slot + u, t * P:(t + 1) * P]
                            first = first_chunk and u == 0
                            end = last and c == steps[-1][0] and u == 1
                            for n, (lhs, w) in enumerate(((hi, w_hi), (hi, w_lo), (lo, w_hi))):
                                for g in range(2):
                                    mm = pe.matmul(bank[2 * t + g][:, :], lhs,
                                                   w[s][:, u * UNIT + g * HALF:u * UNIT + (g + 1) * HALF],
                                                   start=first and n == 0, stop=end and n == 2)
                    if t == NT - 1:
                        mm.then_inc(w_used, len(steps))
                    elif last:
                        mm.then_inc(rows, 1)

            def col_unit(c, it, u, out_bank, tile_done):
                s = c % 2
                todo = []
                for k in range(KD):
                    at = slice(u * UNIT + k * P, u * UNIT + (k + 1) * P)
                    todo += [(w_hi[s][:, at], xt_hi[:, k, :]), (w_hi[s][:, at], xt_lo[:, k, :]),
                             (w_lo[s][:, at], xt_hi[:, k, :])]
                for n, (w, m) in enumerate(todo):
                    if n == 0:
                        pe.wait_ge(lo_ready, 2 * (c + 2 * it) + u + 1)
                    mm = pe.matmul(out_bank[:, :], w, m, start=n == 0, stop=n == len(todo) - 1)
                    if n == len(todo) - 1:
                        mm.then_inc(w_used if u else tile_done, 1)
                    yield mm

            def project(a, b, c, it):
                yield from col_unit(b + AT_QK + c, it, 0, bank[0], a["q_mm"])
                yield from col_unit(b + AT_QK + c, it, 1, bank[1], None)

            def position(l, b, c, it, dense):
                a, i = A[l], c + 2 * it
                par = c % 2
                steps = 8 if l == 0 else 4
                heads = 2 if l == 0 else 1
                per, dense_steps = (8, 6) if l == 0 else (12, 4)
                more = project(a, b, c + 1, it) if dense else iter(())

                def scores(j):
                    h, qi = j // NT, j % NT
                    pe.matmul(bank[2 + j % 2][:, 0:(qi + 1) * P], qa[par][:, h, qi * P:(qi + 1) * P],
                              ka[par][:, 0:(qi + 1) * P], start=True, stop=True).then_inc(a["s_mm"], 1)

                def turn(j):
                    g, qi = steps * i + j, j % NT
                    pe.wait_ge(a["p_ok"], g + 1)
                    if j >= 2:
                        ev, n = (a["tev_v"], j // 2) if j % 2 == 0 else (a["tev_a"], j // 2)
                        pe.wait_ge(ev, steps // 2 * i + n)
                    for kj in range(qi + 1):
                        mm = pe.transpose(bank[4 + j % 2][:, kj * P:(kj + 1) * P],
                                          probs[j % 2][:, kj * P:(kj + 1) * P], ident[:, :])
                    mm.then_inc(a["t_mm"], 1)

                def weigh(h):
                    n = steps * i + NT * (h + 1)
                    pe.wait_ge(a["tev_v"], steps // 2 * i + 2 * (h + 1))
                    pe.wait_ge(a["tev_a"], steps // 2 * i + 2 * (h + 1))
                    if h == 0:
                        pe.wait_ge(a["v_pos"], i + 1)
                    dh = P // heads
                    for kj in range(NT):
                        mm = pe.matmul(bank[6 + par][h * dh:(h + 1) * dh, kj * P:S],
                                       v_pos[par][:, kj, h * dh:(h + 1) * dh],
                                       probs_t[h][:, kj, kj * P:S], start=kj == 0, stop=kj == NT - 1)
                    if h == heads - 1:
                        mm.then_inc(a["pv"], 1)

                pe.wait_ge(a["q_ok"], heads * (i + 1))
                pe.wait_ge(a["k_ok"], i + 1)
                scores(0)
                scores(1)
                for j in range(steps):
                    if dense and j < dense_steps:
                        for _ in range(per):
                            next(more)
                    turn(j)
                    if j + 2 < steps:
                        scores(j + 2)
                    if l == 0 and j == 6:
                        weigh(0)
                weigh(heads - 1)

            pe.wait_ge(const_full, 32)
            turn_x(0)
            for l in range(DEPTH):
                b = l * PER_LAYER
                xt = T[2 * l]

                def x_tile(t):
                    pe.wait_ge(xt["hi"], 2 * t + 2)
                    pe.wait_ge(xt["lo"], 2 * t + 2)

                for c in range(N_V):
                    row_steps([(b + c, 0, 2 * c)], (xt_hi, xt_lo), c == 0, c == N_V - 1, V[l]["rows"],
                              x_tile if c == 0 else lambda t: None)
                pe.wait_ge(V[l]["act"], NT)
                pe.wait_ge(V[l]["dve"], NT)
                for _ in project(A[l], b, 0, 0):
                    pass
                with pe.Fori(0, 3) as it:
                    position(l, b, 0, it, True)
                    position(l, b, 1, it, True)
                position(l, b, 6, 0, True)
                position(l, b, 7, 0, False)
                pe.wait_ge(A[l]["ot_lo"], NPOS)
                for c in range(2):
                    row_steps([(b + AT_O + c, 0, 2 * c)], (a_hi, a_lo), c == 0, False, None, lambda t: None)
                row_steps([(b + AT_O + c, 0, 2 * c) for c in (2, 3)], (a_hi, a_lo), False, True,
                          N[2 * l]["rows"], lambda t: None)
                turn_x(2 * l + 1)
                pe.wait_ge(T[2 * l + 1]["lo"], 2 * NT)

                def up_body(c, it, first):
                    f, u, s = c + 2 * it, U[l], c % 2
                    if not first:
                        pe.wait_ge(u["gc"], f - 1)
                    for _ in col_unit(b + AT_UP + c, it, 0, bank[2 * s], u["g_mm"]):
                        pass
                    if not first:
                        pe.wait_ge(u["vc"], f - 1)
                    for _ in col_unit(b + AT_UP + c, it, 1, bank[2 * s + 1], None):
                        pass

                up_body(0, 0, True)
                up_body(1, 0, True)
                with pe.Fori(1, KF // 2) as it:
                    up_body(0, it, False)
                    up_body(1, it, False)
                pe.wait_ge(U[l]["vc"], KF)

                def down(pairs, first, last):
                    steps = [(b + AT_DN + c, it, 2 * (c % 2)) for c, it in pairs]

                    def chunk(t):
                        if t == 0:
                            for c, it in pairs:
                                pe.wait_ge(DN[l]["a_lo"], c + 2 * it + 1)
                    row_steps(steps, (a_hi, a_lo), first, last, N[2 * l + 1]["rows"], chunk)

                down([(0, 0)], True, False)
                with pe.Fori(0, 4) as it:
                    down([(1, it)], False, False)
                    down([(2, it)], False, False)
                down([(9, 0), (10, 0)], False, True)
                if l < DEPTH - 1:
                    turn_x(2 * l + 2)


def launch_arrays(x, w_qkv_ab, w_o_ab, w_qkv_c, w_o_c, ln_mix_g, ln_mix_b,
                  w_up, conv_w, conv_b, w_down, ln_ffn_g, ln_ffn_b):
    import numpy as np

    def columns(w, tiles):
        w = w.reshape(KD, P, -1, P)
        return np.stack([w[:, :, t, :].transpose(1, 0, 2).reshape(P, D) for t in tiles])

    def steps(units):
        return np.ascontiguousarray(units.reshape(-1, 2, P, UNIT).transpose(0, 2, 1, 3)).reshape(-1, P, 2 * UNIT)

    stream = []
    for l in range(DEPTH):
        order = [2, 3, 4, 5, 6, 7, 0, 1] if l == 0 else list(range(NPOS))
        w_qkv, w_o = (w_qkv_ab[0], w_o_ab[0]) if l == 0 else (w_qkv_c[0], w_o_c[0])
        q, k, v = (w_qkv[:, n * D:(n + 1) * D] for n in range(3))
        v = v.reshape(D, NPOS, P)[:, order].reshape(KD, P, D)
        o = w_o.reshape(NPOS, P, D)[order]
        qk = np.stack([columns(q, order), columns(k, order)], axis=1)
        up = np.stack([columns(w_up[l], range(KF)), columns(w_up[l], range(KF, 2 * KF))], axis=1)
        for part in (v, qk, o, up, w_down[l].reshape(KF, P, D)):
            stream.append(steps(np.ascontiguousarray(part).reshape(-1, P, UNIT)))
    taps = np.concatenate([conv_w, conv_b[:, None]], axis=1)
    taps = taps.reshape(DEPTH, 4, 2 * KF, P).transpose(3, 0, 2, 1)
    ln = np.stack([np.stack([ln_mix_g, ln_mix_b], 1), np.stack([ln_ffn_g, ln_ffn_b], 1)], 1)

    inv = np.float32(1.0) / (np.float32(10000.0) ** (np.arange(0, 64, 2, dtype=np.float32) / np.float32(64)))
    ang = (np.arange(S, dtype=np.float32)[:, None] * inv[None, :]).T
    cos, sin = np.cos(ang), np.sin(ang)
    rope = np.stack([np.tile(cos, (4, 1)), np.concatenate([-sin, sin, -sin, sin])], axis=1)
    dist = 384 + np.arange(P)[:, None] - np.arange(S)[None, :]
    count = (dist >= 0) * ((dist <= 128) * 1 + (dist % 4 == 0) + (dist % 16 == 0))
    dilated = np.where(count > 0, -np.log(np.maximum(count, 1)), FORBID)
    masks = np.stack([dilated, np.where(dist >= 0, 0.0, FORBID)], axis=1)
    tri = np.where(np.arange(P)[None, :] < np.arange(P)[:, None], 0.0, -FORBID)
    f32 = lambda a: np.ascontiguousarray(a, dtype=np.float32)
    return {
        "x_in": x.reshape(S, D), "w_stream": np.concatenate(stream), "ident_in": f32(np.eye(P)),
        "rope_in": f32(rope), "mask_in": f32(masks), "tri_in": f32(tri),
        "conv_in": np.ascontiguousarray(taps).reshape(P, -1), "ln_in": np.ascontiguousarray(ln.reshape(2 * DEPTH, 2, D)),
    }


def kernel(**inputs):
    import numpy as np
    from concourse import bacc
    from concourse.bass_utils import run_bass_kernel_spmd

    arrays = launch_arrays(**{k: np.asarray(v) for k, v in inputs.items()})
    nc = bacc.Bacc("TRN2", target_bir_lowering=False, num_devices=1)
    args = [nc.dram_tensor(name, a.shape, F32, kind="ExternalInput").ap() for name, a in arrays.items()]
    out = nc.dram_tensor("out", (S, D), F32, kind="ExternalOutput").ap()
    build(nc, *args, out)
    r = run_bass_kernel_spmd(nc, [arrays], core_ids=[0])
    return r.results[0]["out"].reshape(1, S, D)
```

```python
from contextlib import ExitStack

import concourse.bass as bass
from concourse import mybir

F32 = mybir.dt.float32
F32R = mybir.dt.float32r
ACT = mybir.ActivationFunctionType
ALU = mybir.AluOpType

P = 128
S, D, DEPTH = 512, 1024, 2
F = ((8 * D // 3 + 127) // 128) * 128
KD = D // P
KF = F // P
NT = S // P
HALF = D // 2
NPOS = 8
ALPHA = (2 * DEPTH) ** 0.25
EPS = 1e-5
SB_SCALE = 128 ** -0.5
MOBA_SCALE = 64 ** -0.5
FORBID = 1e30
UNIT = D

N_V, N_QK, N_O, N_UP, N_DN = KD // 2, NPOS, KD // 2, KF, KF // 2
AT_V = 1
AT_QK = N_V
AT_O = AT_QK + N_QK
AT_UP = AT_O + N_O
AT_DN = AT_UP + N_UP
PER_LAYER = AT_DN + N_DN
STEPS = DEPTH * PER_LAYER


def build(nc, x_in, w_stream, ident_in, rope_in, mask_in, tri_in, conv_in, ln_in, out):
    ctx = ExitStack()
    with ctx:
        def sb(name, shape, dt=F32, stack=ctx):
            return stack.enter_context(nc.sbuf_tensor(name, shape, dt))

        def sem(name):
            return ctx.enter_context(nc.semaphore(name))

        bank = [ctx.enter_context(nc.psum_tensor(f"bank{b}", [P, 512], F32)) for b in range(8)]

        w_raw = [sb(f"w_raw{s}", [P, 2 * UNIT]) for s in range(2)]
        w_hi = [sb(f"w_hi{s}", [P, 2 * UNIT], F32R) for s in range(2)]
        w_lo = [sb(f"w_lo{s}", [P, 2 * UNIT], F32R) for s in range(2)]
        xt_hi = sb("xt_hi", [P, KD, S], F32R)
        xt_lo = sb("xt_lo", [P, KD, S], F32R)
        a_hi = sb("a_hi", [P, KD, S], F32R)
        a_lo = sb("a_lo", [P, KD, S], F32R)
        x = sb("x", [P, NT, D])
        gain = sb("gain", [P, D])
        shift = sb("shift", [P, D])
        ident = sb("ident", [P, P])
        conv = sb("conv", [P, DEPTH * 2 * KF * 4])
        eps = sb("eps", [P, 1])
        stat = sb("stat", [P, NT, 10])

        with ExitStack() as st:
            v_all = sb("v_all", [P, NT, D], stack=st)
            v_pos = [sb(f"v_pos{s}", [P, NT, P], stack=st) for s in range(2)]
            probs_t = [sb(f"probs_t{h}", [P, NT, S], stack=st) for h in range(2)]
            qa = [sb(f"qa{s}", [P, 2, S], stack=st) for s in range(2)]
            ka = [sb(f"ka{s}", [P, S], stack=st) for s in range(2)]
            probs = [sb(f"probs{s}", [P, S], stack=st) for s in range(2)]
            with ExitStack() as ev:
                rope = sb("rope", [P, 2, S], stack=ev)
                masks = sb("masks", [P, 2, S], stack=ev)
                qc = sb("qc", [P, S], stack=ev)
                qs = sb("qs", [P, S], stack=ev)
                kc = sb("kc", [P, S], stack=ev)
                ks = sb("ks", [P, S], stack=ev)
                sm = sb("sm", [P, 2, 4], stack=ev)
            with ExitStack() as od:
                soft = [sb(f"soft{s}", [P, S], stack=od) for s in range(2)]
                tri = sb("tri", [P, P], stack=od)
        with ExitStack() as st:
            h_all = sb("h_all", [P, KF, S], stack=st)
            cg = [sb(f"cg{s}", [P, S], stack=st) for s in range(2)]
            cv = [sb(f"cv{s}", [P, S], stack=st) for s in range(2)]
            sig = [sb(f"sig{s}", [P, S], stack=st) for s in range(2)]
        with ExitStack() as st:
            sb("below_ln", [P, KF, S], stack=st)
            ln_mul = sb("ln_mul", [P, D], stack=st)
            ln_junk = sb("ln_junk", [P, D], stack=st)

        raw_full = [sem(f"raw_full{s}") for s in range(2)]
        first_full = sem("first_full")
        first_hi = sem("first_hi")
        hi_ready = sem("hi_ready")
        lo_ready = sem("lo_ready")
        w_used = sem("w_used")
        x_full = [sem(f"x_full{t}") for t in range(NT)]
        ident_full = sem("ident_full")
        conv_full = sem("conv_full")
        even_full = sem("even_full")
        tri_full = sem("tri_full")
        gb_full = sem("gb_full")
        set_ready = sem("set_ready")
        out_done = sem("out_done")

        def tap(l, tile, k):
            return conv[:, bass.ds((tile + l * 2 * KF) * 4 + k, 1)]

        class Phase:
            def __init__(self, tag, names):
                self.by = {n: sem(f"{tag}_{n}") for n in names.split()}

            def __getitem__(self, n):
                return self.by[n]

        V = [Phase(f"v{l}", "rows act dve") for l in range(DEPTH)]
        A = [Phase(f"a{l}", "q_mm q_cp k_cp q_sw k_sw q_m k_m q_ok k_ok s_mm s_rd ex rc p_ok t_mm "
                            "tev_a tev_v v_pos pv ot_hi ot_lo zm ab e1 ln sp sc rr") for l in range(DEPTH)]
        N = [Phase(f"n{i}", "rows sum mean sq lv y0 va nt mulg xn") for i in range(2 * DEPTH)]
        T = [Phase(f"t{i}", "mm hi lo") for i in range(2 * DEPTH)]
        U = [Phase(f"u{l}", "g_mm cg cv g1 gc sg m1 v1 vc h") for l in range(DEPTH)]
        DN = [Phase(f"d{l}", "a_hi a_lo") for l in range(DEPTH)]

        block = ctx.enter_context(nc.Block())

        def filled(c, it):
            return 16 * (c // 2 + it + 1)

        @block.sync
        def _(sp):
            sp.dma_start(w_raw[0][:, 0:UNIT], w_stream[0, :, 0:UNIT]).then_inc(first_full, 16)
            for t in range(NT):
                sp.dma_start(x[:, t, :], x_in[t * P:(t + 1) * P, :]).then_inc(x_full[t], 16)
                if t == 1:
                    sp.dma_start(w_raw[0][:, UNIT:2 * UNIT], w_stream[0, :, UNIT:2 * UNIT])\
                        .then_inc(raw_full[0], 16)
            sp.dma_start(w_raw[1][:, :], w_stream[1]).then_inc(raw_full[1], 16)

            def load(c, it=0):
                sp.wait_ge(lo_ready, 2 * (c + 2 * it) - 2)
                sp.dma_start(w_raw[c % 2][:, :], w_stream[c + 2 * it]).then_inc(raw_full[c % 2], 16)

            def swap(dst, src, copied, swapped, i):
                sp.wait_ge(copied, i + 1)
                for n in range(2):
                    sp.dma_start(dst[n::2, :], src[1 - n::2, :]).then_inc(swapped, 16)

            def swaps(i):
                swap(qs, qc, A[0]["q_cp"], A[0]["q_sw"], i)
                swap(ks, kc, A[0]["k_cp"], A[0]["k_sw"], i)

            ahead = AT_QK + 3
            for c in range(2, ahead):
                load(c)
                if c == 2:
                    swaps(0)
            with sp.Fori(0, 3) as it:
                for j in range(2):
                    load(ahead + j, it)
                    swaps(2 * it + j + 1)
            load(ahead + 6)
            swaps(7)
            with sp.Fori(0, (STEPS - ahead - 7) // 2) as it:
                for j in range(2):
                    load(ahead + 7 + j, it)
            for t in range(NT):
                sp.wait_ge(N[-1]["xn"], t + 1)
                sp.dma_start(out[t * P:(t + 1) * P, :], x[:, t, :]).then_inc(out_done, 16)
            sp.wait_ge(out_done, 16 * NT)

        @block.gpsimd
        def _(pool):
            def rest(c, it=0, first=False):
                s = c % 2
                for u in range(2):
                    if first and u == 0:
                        pool.wait_ge(first_hi, 1)
                    else:
                        pool.wait_ge(hi_ready, c + 2 * it + 1)
                    part = slice(u * UNIT, (u + 1) * UNIT)
                    pool.tensor_tensor(w_lo[s][:, part], w_raw[s][:, part],
                                       w_hi[s][:, part].bitcast(F32), ALU.subtract).then_inc(lo_ready, 1)

            def rotate_q(slot, i):
                a = A[0]
                pool.wait_ge(a["q_sw"], 32 * (i + 1))
                for n, (t, tab) in enumerate(((qc, 0), (qs, 1))):
                    pool.tensor_tensor(t[:, :], t[:, :], rope[:, tab, :], ALU.mult).then_inc(a["q_m"], 1)
                pool.wait_ge(a["q_m"], 2 * i + 2)
                for h in range(2):
                    part = slice(64 * h, 64 * h + 64)
                    pool.tensor_tensor(qa[slot][part, h, :], qc[part, :], qs[part, :],
                                       ALU.add).then_inc(a["q_ok"], 1)
                    pool.wait_ge(a["q_ok"], 2 * i + h + 1)

            rest(0, first=True)
            for l in range(DEPTH):
                b = l * PER_LAYER
                for c in range(1, AT_QK + 1):
                    rest(b + c)
                    if l == 0 and c == 1:
                        pool.wait_ge(even_full, 32)
                        rotate_q(0, 0)
                for sname in ("act", "dve"):
                    pool.wait_ge(V[l][sname], NT)

                def position(j, it, dense):
                    rest(b + AT_QK + 1 + j, it)
                    pool.wait_ge(w_used, b + AT_QK + 2 * it + j + 1)
                    pool.tensor_copy(v_pos[j % 2][:, :, :], v_all[:, :, bass.ds((2 * it + j) * P, P)])\
                        .then_inc(A[l]["v_pos"], 1)
                    if l == 0 and dense:
                        rotate_q((j + 1) % 2, 2 * it + j + 1)

                with pool.Fori(0, 3) as it:
                    position(0, it, True)
                    position(1, it, True)
                position(6, 0, True)
                position(7, 0, False)
                first = b + AT_O + 1
                n = min(b + PER_LAYER + 1, STEPS) - first
                with pool.Fori(0, n // 2) as it:
                    for j in range(2):
                        rest(first + j, it)
                if n % 2:
                    rest(first + n - 1)

        @block.scalar
        def _(act):
            def heads(c, it=0, used=True):
                act.wait_ge(raw_full[c % 2], filled(c, it))
                if used:
                    act.wait_ge(w_used, c + 2 * it - 1)
                act.activation(w_hi[c % 2][:, :], w_raw[c % 2][:, :], ACT.Copy).then_inc(hi_ready, 1)

            def load_gain(i):
                for row, dst in ((0, gain), (1, shift)):
                    act.dma_start(dst[:, :], ln_in[i, row:row + 1, :].broadcast_to([P, D])).then_inc(gb_full, 16)

            def xt_heads(i, t):
                act.wait_ge(T[i]["mm"], t + 1)
                for g in range(2):
                    act.activation(xt_hi[:, 4 * g:4 * g + 4, t * P:(t + 1) * P],
                                   bank[2 * t + g][:, :].rearrange("p (k q) -> p k q", k=4),
                                   ACT.Copy).then_inc(T[i]["hi"], 1)

            def norm_stats(i, t):
                n = N[i]
                act.wait_ge(n["mean"], t + 1)
                act.activation(ln_junk[:, :], x[:, t, :], ACT.Square, bias=stat[:, t, 2:3],
                               accum_out=stat[:, t, 3:4]).then_inc(n["sq"], 1)
                act.wait_ge(n["sq"], t + 1)
                act.activation(stat[:, t, 4:5], stat[:, t, 3:4], ACT.Ln, bias=eps[:, 0:1],
                               scale=1.0 / D).then_inc(n["lv"], 1)
                act.wait_ge(n["lv"], t + 1)
                act.activation(stat[:, t, 5:6], stat[:, t, 4:5], ACT.Exp, scale=-0.5).then_inc(n["y0"], 1)

            def values(l):
                for t in range(NT):
                    if t < NT - 1:
                        act.wait_ge(V[l]["rows"], t + 1)
                    else:
                        act.wait_ge(w_used, l * PER_LAYER + AT_QK + 1)
                    act.activation(v_all[:, t, 0:HALF], bank[2 * t][:, :], ACT.Copy).then_inc(V[l]["act"], 1)

            def turn_out(a, j, steps, g):
                act.wait_ge(a["t_mm"], g + 1)
                qi = j % NT
                act.activation(probs_t[j // NT][:, 0:qi + 1, qi * P:(qi + 1) * P],
                               bank[4 + j % 2][:, 0:(qi + 1) * P].rearrange("p (k q) -> p k q", q=P),
                               ACT.Copy).then_inc(a["tev_a"], 1)

            def out_heads(a, i, slot):
                act.wait_ge(a["pv"], i + 1)
                act.activation(a_hi[:, bass.ds(i, 1), :],
                               bank[6 + slot][:, :].rearrange("p (a q) -> p a q", a=1),
                               ACT.Copy).then_inc(a["ot_hi"], 1)

            def even_body(b, c, it, dense, before):
                a = A[0]
                i = c + 2 * it
                for j in range(8):
                    g = 8 * i + j
                    if j == 2:
                        if before:
                            out_heads(a, i - 1, (c - 1) % 2)
                        heads(b + AT_QK + c + 2, it)
                    if j % 2 == 1 and j >= 3:
                        turn_out(a, j - 2, 8, g - 2)
                    if j == 4 and dense:
                        act.wait_ge(a["q_mm"], i + 2)
                        act.activation(qc[:, :], bank[0][:, :], ACT.Copy, scale=-MOBA_SCALE).then_inc(a["q_cp"], 1)
                    if j == 7 and dense:
                        act.wait_ge(w_used, b + AT_QK + i + 2)
                        act.activation(kc[:, :], bank[1][:, :], ACT.Copy).then_inc(a["k_cp"], 1)
                    act.wait_ge(a["s_rd"], g + 1)
                    L = (j % NT + 1) * P
                    act.activation(probs[j % 2][:, 0:L], probs[j % 2][:, 0:L], ACT.Exp,
                                   bias=sm[:, j % 2, 0:1], scale=-1.0,
                                   accum_out=sm[:, j % 2, 1:2]).then_inc(a["ex"], 1)
                turn_out(a, 7, 8, 8 * i + 7)

            def odd_body(b, c, it, dense, before):
                a = A[1]
                i = c + 2 * it

                def soft_part(j):
                    g, L = 4 * i + j, (j + 1) * P
                    e = soft[j % 2][:, 0:L]
                    act.wait_ge(a["zm"], g + 1)
                    act.activation(e, bank[2 + j % 2][:, 0:L], ACT.Abs).then_inc(a["ab"], 1)
                    act.wait_ge(a["ab"], g + 1)
                    act.activation(e, e, ACT.Exp, scale=-1.0).then_inc(a["e1"], 1)
                    act.wait_ge(a["e1"], g + 1)
                    act.activation(e, e, ACT.Ln, bias=1.0).then_inc(a["ln"], 1)

                def weight_part(j):
                    g, L = 4 * i + j, (j + 1) * P
                    act.wait_ge(a["rr"], g + 1)
                    act.activation(probs[j % 2][:, 0:L], probs[j % 2][:, 0:L], ACT.Exp).then_inc(a["p_ok"], 1)

                for j in range(4):
                    if j == 2:
                        if before:
                            out_heads(a, i - 1, (c - 1) % 2)
                        heads(b + AT_QK + c + 2, it)
                    if j == 3:
                        turn_out(a, 1, 4, 4 * i + 1)
                        if dense:
                            act.wait_ge(a["q_mm"], i + 2)
                            act.activation(qa[(c + 1) % 2][:, 0, :], bank[0][:, :], ACT.Copy,
                                           scale=SB_SCALE).then_inc(a["q_ok"], 1)
                    soft_part(j)
                    if j >= 1:
                        weight_part(j - 1)
                weight_part(3)
                if dense:
                    act.wait_ge(w_used, b + AT_QK + i + 2)
                    act.activation(ka[(c + 1) % 2][:, :], bank[1][:, :], ACT.Copy).then_inc(a["k_ok"], 1)
                turn_out(a, 3, 4, 4 * i + 3)

            act.dma_start(ident[:, :], ident_in).then_inc(ident_full, 16)
            act.dma_start(conv[:, :], conv_in).then_inc(conv_full, 16)
            act.dma_start(rope[:, :, :], rope_in).then_inc(even_full, 16)
            act.dma_start(masks[:, :, :], mask_in).then_inc(even_full, 16)
            load_gain(0)
            act.preload_act_table_set("natural_log_exp_and_others")
            act.wait_ge(first_full, 16)
            act.activation(w_hi[0][:, 0:UNIT], w_raw[0][:, 0:UNIT], ACT.Copy).then_inc(first_hi, 1)
            act.wait_ge(set_ready, 5)
            xt_heads(0, 0)
            xt_heads(0, 1)
            act.wait_ge(raw_full[0], 16)
            act.activation(w_hi[0][:, UNIT:2 * UNIT], w_raw[0][:, UNIT:2 * UNIT], ACT.Copy)\
                .then_inc(hi_ready, 1)
            xt_heads(0, 2)
            xt_heads(0, 3)
            heads(1, used=False)

            for l in range(DEPTH):
                b = l * PER_LAYER
                if l == 0:
                    a = A[0]
                    act.wait_ge(a["q_mm"], 1)
                    act.activation(qc[:, :], bank[0][:, :], ACT.Copy, scale=-MOBA_SCALE).then_inc(a["q_cp"], 1)
                    act.wait_ge(w_used, b + 1)
                    act.activation(kc[:, :], bank[1][:, :], ACT.Copy).then_inc(a["k_cp"], 1)
                    body = even_body
                else:
                    a = A[1]
                    act.wait_ge(N[1]["xn"], NT)
                    act.dma_start(tri[:, :], tri_in).then_inc(tri_full, 16)
                    act.wait_ge(a["q_mm"], 1)
                    act.activation(qa[0][:, 0, :], bank[0][:, :], ACT.Copy, scale=SB_SCALE).then_inc(a["q_ok"], 1)
                    act.wait_ge(w_used, b + 1)
                    act.activation(ka[0][:, :], bank[1][:, :], ACT.Copy).then_inc(a["k_ok"], 1)
                    body = odd_body
                for c in range(2, AT_QK + 2):
                    heads(b + c)
                values(l)
                body(b, 0, 0, True, False)
                with act.Fori(0, 3) as it:
                    body(b, 1, it, True, True)
                    body(b, 2, it, True, True)
                body(b, 7, 0, False, True)
                out_heads(A[l], 7, 1)
                for c in range(2):
                    heads(b + AT_O + 2 + c)
                for i, after in ((2 * l, b + AT_O + 4), (2 * l + 1, b + PER_LAYER)):
                    if i % 2:
                        def chunk_heads(c, it=0, used=True):
                            j = c + 2 * it
                            act.wait_ge(U[l]["h"], 2 * j + 2)
                            if used:
                                act.wait_ge(w_used, b + AT_DN + j - 1)
                            act.activation(a_hi[:, 2 * (c % 2):2 * (c % 2) + 2, :],
                                           h_all[:, bass.ds(2 * j, 2), :], ACT.Copy).then_inc(DN[l]["a_hi"], 1)

                        def up_body(c, it, first):
                            f, u = c + 2 * it, U[l]
                            s = c % 2
                            act.wait_ge(u["g_mm"], f + 1)
                            if not first:
                                act.wait_ge(u["h"], f - 1)
                            act.activation(cg[s][:, :], bank[2 * s][:, :], ACT.Identity,
                                           bias=tap(l, f, 3),
                                           scale=tap(l, f, 2)).then_inc(u["cg"], 1)
                            heads(b + AT_UP + c + 2, it)
                            act.wait_ge(u["gc"], f + 1)
                            act.activation(sig[s][:, :], cg[s][:, :], ACT.Sigmoid).then_inc(u["sg"], 1)
                            act.wait_ge(w_used, b + AT_UP + f + 1)
                            act.activation(cv[s][:, :], bank[2 * s + 1][:, :], ACT.Identity,
                                           bias=tap(l, f + KF, 3),
                                           scale=tap(l, f + KF, 2)).then_inc(u["cv"], 1)

                        act.preload_act_table(ACT.Sigmoid)
                        act.wait_ge(conv_full, 16)
                        up_body(0, 0, True)
                        up_body(1, 0, True)
                        chunk_heads(0, used=False)
                        with act.Fori(1, KF // 2) as it:
                            up_body(0, it, False)
                            up_body(1, it, False)

                        act.preload_act_table_set("natural_log_exp_and_others")
                        chunk_heads(1)
                        chunk_heads(2)
                        heads(b + AT_DN + 2)
                        with act.Fori(0, 4) as it:
                            for j in (1, 2):
                                chunk_heads(j + 2, it)
                                heads(b + AT_DN + 2 + j, it)
                    turn = i < 2 * DEPTH - 1
                    for t in range(NT):
                        if t == NT - 1 and turn:
                            xt_heads(i + 1, 0)
                            xt_heads(i + 1, 1)
                            heads(after)
                        norm_stats(i, t)
                    if turn:
                        xt_heads(i + 1, 2)
                        xt_heads(i + 1, 3)
                    if i < 2 * DEPTH - 1:
                        heads(after + 1)
                        act.wait_ge(N[i]["xn"], NT)
                        load_gain(i + 1)

        @block.vector
        def _(dve):
            def xt_rests(i, t):
                dve.wait_ge(T[i]["hi"], 2 * t + 2)
                for g in range(2):
                    part = xt_hi[:, 4 * g:4 * g + 4, t * P:(t + 1) * P]
                    dve.tensor_tensor(xt_lo[:, 4 * g:4 * g + 4, t * P:(t + 1) * P],
                                      bank[2 * t + g][:, :].rearrange("p (k q) -> p k q", k=4),
                                      part.bitcast(F32), ALU.subtract).then_inc(T[i]["lo"], 1)

            def norm_a(i, t):
                n = N[i]
                if t < NT - 1:
                    dve.wait_ge(n["rows"], t + 1)
                else:
                    dve.wait_ge(w_used, i // 2 * PER_LAYER + (PER_LAYER if i % 2 else AT_UP))
                for g in range(2):
                    dve.scalar_tensor_tensor(out=x[:, t, g * HALF:(g + 1) * HALF],
                                             in0=x[:, t, g * HALF:(g + 1) * HALF], scalar=ALPHA,
                                             in1=bank[2 * t + g][:, :], op0=ALU.mult, op1=ALU.add,
                                             accum_out=stat[:, t, g:g + 1]).then_inc(n["sum"], 1)
                dve.wait_ge(n["sum"], 2 * t + 2)
                dve.tensor_scalar(stat[:, t, 2:3], stat[:, t, 0:1], stat[:, t, 1:2], -1.0 / D,
                                  ALU.add, ALU.mult).then_inc(n["mean"], 1)
                dve.wait_ge(n["mean"], t + 1)
                if t == 0:
                    dve.wait_ge(gb_full, 32 * (i + 1))
                else:
                    dve.wait_ge(n["xn"], t)
                dve.scalar_tensor_tensor(out=ln_mul[:, :], in0=x[:, t, :], scalar=stat[:, t, 2:3],
                                         in1=gain[:, :], op0=ALU.add, op1=ALU.mult).then_inc(n["mulg"], 1)

            def norm_b(i, t):
                n = N[i]
                v, y0, w, r = (stat[:, t, k:k + 1] for k in (6, 5, 7, 8))
                dve.wait_ge(n["sq"], t + 1)
                dve.tensor_scalar(v, stat[:, t, 3:4], 1.0 / D, EPS, ALU.mult, ALU.add).then_inc(n["va"], 1)
                dve.wait_ge(n["va"], t + 1)
                dve.wait_ge(n["y0"], t + 1)
                dve.scalar_tensor_tensor(out=w, in0=y0, scalar=v, in1=y0, op0=ALU.mult,
                                         op1=ALU.mult).then_inc(n["nt"], 1)
                dve.wait_ge(n["nt"], 3 * t + 1)
                dve.tensor_scalar(w, w, -0.5, 1.5, ALU.mult, ALU.add).then_inc(n["nt"], 1)
                dve.wait_ge(n["nt"], 3 * t + 2)
                dve.tensor_tensor(r, y0, w, ALU.mult).then_inc(n["nt"], 1)
                dve.wait_ge(n["nt"], 3 * t + 3)
                dve.wait_ge(n["mulg"], t + 1)
                dve.scalar_tensor_tensor(out=x[:, t, :], in0=ln_mul[:, :], scalar=r, in1=shift[:, :],
                                         op0=ALU.mult, op1=ALU.add).then_inc(n["xn"], 1)

            def norm(i):
                turn = i < 2 * DEPTH - 1
                for t in range(NT):
                    if t == NT - 1 and turn:
                        xt_rests(i + 1, 0)
                        xt_rests(i + 1, 1)
                    norm_a(i, t)
                    norm_b(i, t)
                if turn:
                    xt_rests(i + 1, 2)
                    xt_rests(i + 1, 3)

            def rope_k(a, s, i):
                dve.wait_ge(a["k_cp"], i + 1)
                dve.tensor_tensor(ka[s][:, :], kc[:, :], rope[:, 0, :], ALU.mult).then_inc(a["k_m"], 1)
                dve.wait_ge(a["k_sw"], 32 * (i + 1))
                dve.tensor_tensor(ks[:, :], ks[:, :], rope[:, 1, :], ALU.mult).then_inc(a["k_m"], 1)
                dve.wait_ge(a["k_m"], 2 * i + 2)
                dve.tensor_tensor(ka[s][:, :], ka[s][:, :], ks[:, :], ALU.add).then_inc(a["k_ok"], 1)

            def turn_out(a, j, g):
                dve.wait_ge(a["t_mm"], g + 1)
                qi = j % NT
                dve.tensor_copy(probs_t[j // NT][:, 0:qi + 1, qi * P:(qi + 1) * P],
                                bank[4 + j % 2][:, 0:(qi + 1) * P].rearrange("p (k q) -> p k q", q=P))\
                    .then_inc(a["tev_v"], 1)

            def out_rests(a, i, par):
                dve.wait_ge(a["ot_hi"], i + 1)
                dve.tensor_tensor(a_lo[:, bass.ds(i, 1), :],
                                  bank[6 + par][:, :].rearrange("p (a q) -> p a q", a=1),
                                  a_hi[:, bass.ds(i, 1), :].bitcast(F32), ALU.subtract).then_inc(a["ot_lo"], 1)

            def even_body(c, it, dense, before, kind):
                a, i = A[0], c + 2 * it

                def bound(j):
                    g, qi = 8 * i + j, j % NT
                    L = (qi + 1) * P
                    dve.wait_ge(a["s_mm"], g + 1)
                    dve.memset(sm[:, j % 2, 3:4], 0.0)
                    dve.tensor_tensor_reduce(probs[j % 2][:, 0:L], bank[2 + j % 2][:, 0:L],
                                             masks[:, kind, S - L:S], 1.0, 3e38, ALU.add, ALU.min,
                                             sm[:, j % 2, 0:1]).then_inc(a["s_rd"], 1)

                def divide(j):
                    g, L = 8 * i + j, (j % NT + 1) * P
                    dve.wait_ge(a["ex"], g + 1)
                    dve.reciprocal(sm[:, j % 2, 2:3], sm[:, j % 2, 1:2]).then_inc(a["rc"], 1)
                    dve.wait_ge(a["rc"], g + 1)
                    dve.tensor_scalar(probs[j % 2][:, 0:L], probs[j % 2][:, 0:L], sm[:, j % 2, 2:3], None,
                                      ALU.mult).then_inc(a["p_ok"], 1)

                for j in range(8):
                    if j >= 2 and j % 2 == 0:
                        turn_out(a, j - 2, 8 * i + j - 2)
                    if j >= 2:
                        divide(j - 1)
                    bound(j)
                    if j == 1:
                        divide(0)
                    if j == 2 and before:
                        out_rests(a, i - 1, (c - 1) % 2)
                divide(7)
                turn_out(a, 6, 8 * i + 6)
                if dense:
                    rope_k(a, (c + 1) % 2, i + 1)

            def odd_body(c, it, dense, before, kind):
                a, i = A[1], c + 2 * it

                def mask_diagonal(j):
                    dve.wait_ge(a["s_mm"], 4 * i + j + 1)
                    z = bank[2 + j % 2][:, j * P:(j + 1) * P]
                    dve.tensor_tensor(z, z, tri[:, :], ALU.add).then_inc(a["zm"], 1)

                def break_stick(j):
                    g, L = 4 * i + j, (j + 1) * P
                    z, e, r = bank[2 + j % 2][:, 0:L], soft[j % 2], probs[j % 2]
                    dve.wait_ge(a["ln"], g + 1)
                    dve.scalar_tensor_tensor(out=e[:, 0:L], in0=z, scalar=0.0, in1=e[:, 0:L],
                                             op0=ALU.max, op1=ALU.add).then_inc(a["sp"], 1)
                    dve.wait_ge(a["sp"], g + 1)
                    back = e[:, L - 1::-1]
                    dve.tensor_tensor_scan(r[:, L - 1::-1], back, back, 0.0, ALU.add,
                                           ALU.max).then_inc(a["sc"], 1)
                    dve.wait_ge(a["sc"], g + 1)
                    dve.tensor_tensor(r[:, 0:L], z, r[:, 0:L], ALU.subtract).then_inc(a["rr"], 1)

                for j in range(4):
                    if j == 2:
                        turn_out(a, 0, 4 * i)
                    mask_diagonal(j)
                    if j >= 1:
                        break_stick(j - 1)
                    if j == 2 and before:
                        out_rests(a, i - 1, (c - 1) % 2)
                break_stick(3)
                turn_out(a, 2, 4 * i + 2)

            dve.memset(eps[:, :], EPS).then_inc(set_ready, 1)
            for s in range(2):
                dve.memset(qa[s][P // 2:P, 0, :], 0.0).then_inc(set_ready, 1)
                dve.memset(qa[s][0:P // 2, 1, :], 0.0).then_inc(set_ready, 1)
            dve.wait_ge(set_ready, 5)
            for t in range(NT):
                xt_rests(0, t)
            for l in range(DEPTH):
                if l == 0:
                    a = A[0]
                    dve.wait_ge(even_full, 32)
                    rope_k(a, 0, 0)
                    body = even_body
                else:
                    dve.wait_ge(tri_full, 16)
                    body = odd_body
                for t in range(NT):
                    if t < NT - 1:
                        dve.wait_ge(V[l]["rows"], t + 1)
                    else:
                        dve.wait_ge(w_used, l * PER_LAYER + AT_QK + 1)
                    dve.tensor_copy(v_all[:, t, HALF:D], bank[2 * t + 1][:, :]).then_inc(V[l]["dve"], 1)
                body(0, 0, True, False, 1)
                with dve.Fori(0, 3) as it:
                    body(1, it, True, True, 0)
                    body(2, it, True, True, 0)
                body(7, 0, False, True, 1)
                out_rests(A[l], 7, 1)
                norm(2 * l)

                def up_body(c, it):
                    f, u, s = c + 2 * it, U[l], c % 2

                    def convolve(ps, acc, tile, start, mid, end):
                        dve.wait_ge(start, f + 1)
                        dve.scalar_tensor_tensor(out=acc[:, 1:S], in0=ps[:, 0:S - 1],
                                                 scalar=tap(l, tile, 1), in1=acc[:, 1:S],
                                                 op0=ALU.mult, op1=ALU.add).then_inc(mid, 1)
                        dve.wait_ge(mid, f + 1)
                        dve.scalar_tensor_tensor(out=acc[:, 2:S], in0=ps[:, 0:S - 2],
                                                 scalar=tap(l, tile, 0), in1=acc[:, 2:S],
                                                 op0=ALU.mult, op1=ALU.add).then_inc(end, 1)

                    convolve(bank[2 * s], cg[s], f, u["cg"], u["g1"], u["gc"])
                    dve.wait_ge(u["sg"], f + 1)
                    dve.tensor_tensor(sig[s][:, :], sig[s][:, :], cg[s][:, :], ALU.mult).then_inc(u["m1"], 1)
                    convolve(bank[2 * s + 1], cv[s], f + KF, u["cv"], u["v1"], u["vc"])
                    dve.wait_ge(u["vc"], f + 1)
                    dve.wait_ge(u["m1"], f + 1)
                    dve.tensor_tensor(h_all[:, bass.ds(f, 1), :],
                                      sig[s][:, :].rearrange("p (a q) -> p a q", a=1),
                                      cv[s][:, :].rearrange("p (a q) -> p a q", a=1), ALU.mult).then_inc(u["h"], 1)

                def chunk_rests(c, it=0):
                    j = c + 2 * it
                    dve.wait_ge(DN[l]["a_hi"], j + 1)
                    k = 2 * (c % 2)
                    dve.tensor_tensor(a_lo[:, k:k + 2, :], h_all[:, bass.ds(2 * j, 2), :],
                                      a_hi[:, k:k + 2, :].bitcast(F32), ALU.subtract).then_inc(DN[l]["a_lo"], 1)

                dve.wait_ge(conv_full, 16)
                up_body(0, 0)
                up_body(1, 0)
                chunk_rests(0)
                with dve.Fori(1, KF // 2) as it:
                    up_body(0, it)
                    up_body(1, it)
                with dve.Fori(0, N_DN // 2) as it:
                    chunk_rests(1, it)
                    chunk_rests(2, it)
                norm(2 * l + 1)

        @block.tensor
        def _(pe):
            def turn_x(i, t):
                if i == 0:
                    pe.wait_ge(x_full[t], 16)
                else:
                    pe.wait_ge(N[i - 1]["xn"], t + 1)
                for k in range(KD):
                    mm = pe.transpose(bank[2 * t + k // 4][:, (k % 4) * P:(k % 4 + 1) * P],
                                      x[:, t, k * P:(k + 1) * P], ident[:, :])
                mm.then_inc(T[i]["mm"], 1)

            def row_tiles(steps, a, first_chunk, last, rows, before=None, tiles=range(NT), partial=False):
                for t in tiles:
                    if before:
                        before(t, None)
                    for c, it, slot in steps:
                        if before and c != steps[0][0]:
                            before(t, c)
                        s = c % 2
                        for u in range(2):
                            if t == tiles[0]:
                                pe.wait_ge(lo_ready, 2 * (c + 2 * it) + u + 1)
                            hi = a[0][:, slot + u, t * P:(t + 1) * P]
                            lo = a[1][:, slot + u, t * P:(t + 1) * P]
                            first = first_chunk and c == steps[0][0] and u == 0
                            end = last and c == steps[-1][0] and u == 1
                            frees = t == tiles[-1] and u == 1 and not partial
                            for n, (lhs, w) in enumerate(((hi, w_hi), (hi, w_lo), (lo, w_hi))):
                                for g in range(2):
                                    mm = pe.matmul(bank[2 * t + g][:, :], lhs,
                                                   w[s][:, u * UNIT + g * HALF:u * UNIT + (g + 1) * HALF],
                                                   start=first and n == 0, stop=end and n == 2)
                                    if n == 2 and g == 1:
                                        if frees:
                                            mm.then_inc(w_used, 1)
                                        elif end:
                                            mm.then_inc(rows, 1)
                                    yield mm

            def row_steps(*args, **kw):
                for _ in row_tiles(*args, **kw):
                    pass

            def col_unit(c, it, u, out_bank, tile_done, half=None):
                s = c % 2
                tok = slice(0, S) if half is None else slice(half * S // 2, (half + 1) * S // 2)
                todo = []
                for k in range(KD):
                    at = slice(u * UNIT + k * P, u * UNIT + (k + 1) * P)
                    todo += [(w_hi[s][:, at], xt_hi[:, k, tok]), (w_hi[s][:, at], xt_lo[:, k, tok]),
                             (w_lo[s][:, at], xt_hi[:, k, tok])]
                for n, (w, m) in enumerate(todo):
                    if n == 0:
                        pe.wait_ge(lo_ready, 2 * (c + 2 * it) + u + 1)
                    mm = pe.matmul(out_bank[:, tok], w, m, start=n == 0, stop=n == len(todo) - 1)
                    if n == len(todo) - 1 and half != 0:
                        mm.then_inc(w_used if u else tile_done, 1)
                    yield mm

            def first_columns(c, bank0, signal, i):
                for half in range(2):
                    for unit in range(2):
                        if (half, unit) == (0, 1):
                            turn_x(i, 3)
                        if unit == 0:
                            pe.wait_ge(T[i]["lo"], NT * (half + 1))
                        for _ in col_unit(c, 0, unit, bank[bank0 + unit], signal, half):
                            pass

            def project(a, b, c, it):
                yield from col_unit(b + AT_QK + c, it, 0, bank[0], a["q_mm"])
                yield from col_unit(b + AT_QK + c, it, 1, bank[1], None)

            def position(l, b, c, it, dense, filler=None):
                a, i = A[l], c + 2 * it
                par = c % 2
                steps = 8 if l == 0 else 4
                heads = 2 if l == 0 else 1
                more = project(a, b, c + 1, it) if dense else filler
                if dense:
                    share = (8, 8, 8, 8, 8, 8, 0, 0) if l == 0 else (14, 12, 11, 8)
                else:
                    share = (3,) * 8 if l == 0 else (6,) * 4

                def scores(j):
                    h, qi = j // NT, j % NT
                    pe.matmul(bank[2 + j % 2][:, 0:(qi + 1) * P], qa[par][:, h, qi * P:(qi + 1) * P],
                              ka[par][:, 0:(qi + 1) * P], start=True, stop=True).then_inc(a["s_mm"], 1)

                def turn(j):
                    g, qi = steps * i + j, j % NT
                    pe.wait_ge(a["p_ok"], g + 1)
                    if j >= 2:
                        ev, n = (a["tev_v"], j // 2) if j % 2 == 0 else (a["tev_a"], j // 2)
                        pe.wait_ge(ev, steps // 2 * i + n)
                    for kj in range(qi + 1):
                        mm = pe.transpose(bank[4 + j % 2][:, kj * P:(kj + 1) * P],
                                          probs[j % 2][:, kj * P:(kj + 1) * P], ident[:, :])
                    mm.then_inc(a["t_mm"], 1)

                def weigh(h, keys=range(NT)):
                    pe.wait_ge(a["tev_v"], steps // 2 * i + 2 * (h + 1))
                    pe.wait_ge(a["tev_a"], steps // 2 * i + 2 * (h + 1))
                    if h == 0:
                        pe.wait_ge(a["v_pos"], i + 1)
                    dh = P // heads
                    for kj in keys:
                        mm = pe.matmul(bank[6 + par][h * dh:(h + 1) * dh, kj * P:S],
                                       v_pos[par][:, kj, h * dh:(h + 1) * dh],
                                       probs_t[h][:, kj, kj * P:S], start=kj == 0, stop=kj == NT - 1)
                    if h == heads - 1 and kj == NT - 1:
                        mm.then_inc(a["pv"], 1)

                pe.wait_ge(a["q_ok"], heads * (i + 1))
                pe.wait_ge(a["k_ok"], i + 1)
                scores(0)
                scores(1)
                for j in range(steps):
                    for _ in range(share[j]):
                        next(more)
                    turn(j)
                    if j + 2 < steps:
                        scores(j + 2)
                    if l == 0 and j == 6:
                        weigh(0, (0, 1))
                    if l == 0 and j == 7:
                        weigh(0, (2, 3))
                for _ in more:
                    pass
                weigh(heads - 1)

            pe.wait_ge(ident_full, 16)
            for t in range(NT - 1):
                turn_x(0, t)
            for l in range(DEPTH):
                b = l * PER_LAYER
                def turning(i):
                    def before(t, c):
                        if t == NT - 1:
                            turn_x(i, 0 if c is None else 1)
                    return before

                first_columns(b, 0, A[l]["q_mm"], 2 * l)

                def first_v(t, _):
                    if t == 0:
                        if l == 0:
                            pe.wait_ge(A[l]["q_cp"], 1)
                            pe.wait_ge(A[l]["k_cp"], 1)
                        else:
                            pe.wait_ge(A[l]["q_ok"], 1)
                            pe.wait_ge(A[l]["k_ok"], 1)

                for c in range(N_V):
                    row_steps([(b + AT_V + c, 0, 2 * c)], (xt_hi, xt_lo), c == 0, c == N_V - 1, V[l]["rows"],
                              first_v if c == 0 else None, (1, 2, 3, 0) if c == 0 else range(NT))
                pe.wait_ge(V[l]["act"], NT)
                pe.wait_ge(V[l]["dve"], NT)
                position(l, b, 0, 0, True)
                with pe.Fori(0, 3) as it:
                    position(l, b, 1, it, True)
                    position(l, b, 2, it, True)
                early = [(b + AT_O + c, 0, 2 * c) for c in range(2)]
                position(l, b, 7, 0, False, row_tiles(early, (a_hi, a_lo), True, False, None,
                                                      tiles=(0,), partial=True))
                pe.wait_ge(A[l]["ot_lo"], 2 * 2)

                def last_output(t, _):
                    if t == 3:
                        pe.wait_ge(A[l]["ot_lo"], NPOS)
                row_steps(early, (a_hi, a_lo), True, False, None, last_output, (1, 2, 3))
                row_steps([(b + AT_O + c, 0, 2 * c) for c in (2, 3)], (a_hi, a_lo), False, True,
                          N[2 * l]["rows"], turning(2 * l + 1))
                turn_x(2 * l + 1, 2)

                def up_body(c, it, first):
                    f, u, s = c + 2 * it, U[l], c % 2
                    if not first:
                        pe.wait_ge(u["gc"], f - 1)
                    for _ in col_unit(b + AT_UP + c, it, 0, bank[2 * s], u["g_mm"]):
                        pass
                    if not first:
                        pe.wait_ge(u["vc"], f - 1)
                    for _ in col_unit(b + AT_UP + c, it, 1, bank[2 * s + 1], None):
                        pass

                first_columns(b + AT_UP, 0, U[l]["g_mm"], 2 * l + 1)
                up_body(1, 0, True)
                with pe.Fori(1, KF // 2) as it:
                    up_body(0, it, False)
                    up_body(1, it, False)

                def down(pairs, first, last):
                    steps = [(b + AT_DN + c, it, 2 * (c % 2)) for c, it in pairs]

                    turn = turning(2 * l + 2) if last and l < DEPTH - 1 else None

                    def chunk(t, c):
                        if turn:
                            turn(t, c)
                        if first and t == 0:
                            pe.wait_ge(U[l]["vc"], KF - 1)
                        if first and t == 1:
                            pe.wait_ge(U[l]["vc"], KF)
                        if t == 0 and c is None:
                            for c, it in pairs:
                                pe.wait_ge(DN[l]["a_lo"], c + 2 * it + 1)
                    row_steps(steps, (a_hi, a_lo), first, last, N[2 * l + 1]["rows"], chunk)

                down([(0, 0)], True, False)
                with pe.Fori(0, 4) as it:
                    down([(1, it)], False, False)
                    down([(2, it)], False, False)
                down([(9, 0), (10, 0)], False, True)
                if l < DEPTH - 1:
                    turn_x(2 * l + 2, 2)


def launch_arrays(x, w_qkv_ab, w_o_ab, w_qkv_c, w_o_c, ln_mix_g, ln_mix_b,
                  w_up, conv_w, conv_b, w_down, ln_ffn_g, ln_ffn_b):
    import numpy as np

    def columns(w, tiles):
        w = w.reshape(KD, P, -1, P)
        return np.stack([w[:, :, t, :].transpose(1, 0, 2).reshape(P, D) for t in tiles])

    def steps(units):
        return np.ascontiguousarray(units.reshape(-1, 2, P, UNIT).transpose(0, 2, 1, 3)).reshape(-1, P, 2 * UNIT)

    stream = []
    for l in range(DEPTH):
        order = [0, 2, 3, 4, 5, 6, 7, 1] if l == 0 else list(range(NPOS))
        w_qkv, w_o = (w_qkv_ab[0], w_o_ab[0]) if l == 0 else (w_qkv_c[0], w_o_c[0])
        q, k, v = (w_qkv[:, n * D:(n + 1) * D] for n in range(3))
        v = v.reshape(D, NPOS, P)[:, order].reshape(KD, P, D)
        o = w_o.reshape(NPOS, P, D)[order]
        if l == 0:
            q, k = (w.reshape(D, 16, 2, 32).transpose(0, 1, 3, 2).reshape(D, D) for w in (q, k))
        qk = np.stack([columns(q, order), columns(k, order)], axis=1)
        up = np.stack([columns(w_up[l], range(KF)), columns(w_up[l], range(KF, 2 * KF))], axis=1)
        for part in (qk[:1], v, qk[1:], o, up, w_down[l].reshape(KF, P, D)):
            stream.append(steps(np.ascontiguousarray(part).reshape(-1, P, UNIT)))
    taps = np.concatenate([conv_w, conv_b[:, None]], axis=1)
    taps = taps.reshape(DEPTH, 4, 2 * KF, P).transpose(3, 0, 2, 1)
    ln = np.stack([np.stack([ln_mix_g, ln_mix_b], 1), np.stack([ln_ffn_g, ln_ffn_b], 1)], 1)

    inv = np.float32(1.0) / (np.float32(10000.0) ** (np.arange(0, 64, 2, dtype=np.float32) / np.float32(64)))
    ang = (np.arange(S, dtype=np.float32)[:, None] * inv[None, :]).T
    cos, sin = np.cos(ang), np.sin(ang)
    sin = np.stack([-sin, sin], axis=1).reshape(64, S)
    rope = np.stack([np.tile(np.repeat(cos, 2, axis=0), (2, 1)), np.tile(sin, (2, 1))], axis=1)
    dist = 384 + np.arange(P)[:, None] - np.arange(S)[None, :]
    count = (dist >= 0) * ((dist <= 128) * 1 + (dist % 4 == 0) + (dist % 16 == 0))
    dilated = np.where(count > 0, -np.log(np.maximum(count, 1)), FORBID)
    masks = np.stack([dilated, np.where(dist >= 0, 0.0, FORBID)], axis=1)
    tri = np.where(np.arange(P)[None, :] < np.arange(P)[:, None], 0.0, -FORBID)
    f32 = lambda a: np.ascontiguousarray(a, dtype=np.float32)
    return {
        "x_in": x.reshape(S, D), "w_stream": np.concatenate(stream), "ident_in": f32(np.eye(P)),
        "rope_in": f32(rope), "mask_in": f32(masks), "tri_in": f32(tri),
        "conv_in": np.ascontiguousarray(taps).reshape(P, -1), "ln_in": np.ascontiguousarray(ln.reshape(2 * DEPTH, 2, D)),
    }


def kernel(**inputs):
    import numpy as np
    from concourse import bacc
    from concourse.bass_utils import run_bass_kernel_spmd

    arrays = launch_arrays(**{k: np.asarray(v) for k, v in inputs.items()})
    nc = bacc.Bacc("TRN2", target_bir_lowering=False, num_devices=1)
    args = [nc.dram_tensor(name, a.shape, F32, kind="ExternalInput").ap() for name, a in arrays.items()]
    out = nc.dram_tensor("out", (S, D), F32, kind="ExternalOutput").ap()
    build(nc, *args, out)
    r = run_bass_kernel_spmd(nc, [arrays], core_ids=[0])
    return r.results[0]["out"].reshape(1, S, D)
```

```python
from contextlib import ExitStack
from itertools import chain

import concourse.bass as bass
from concourse import mybir

F32 = mybir.dt.float32
F32R = mybir.dt.float32r
ACT = mybir.ActivationFunctionType
ALU = mybir.AluOpType

P = 128
S, D, DEPTH = 512, 1024, 2
F = ((8 * D // 3 + 127) // 128) * 128
KD = D // P
KF = F // P
NT = S // P
HALF = D // 2
NPOS = 8
ALPHA = (2 * DEPTH) ** 0.25
EPS = 1e-5
SB_SCALE = 128 ** -0.5
MOBA_SCALE = 64 ** -0.5
FORBID = 1e30
UNIT = D

N_V, N_QK, N_O, N_UP, N_DN = KD // 2, NPOS, KD // 2, KF, KF // 2
AT_V = 1
AT_QK = N_V
AT_O = AT_QK + N_QK
AT_UP = AT_O + N_O
AT_DN = AT_UP + N_UP
PER_LAYER = AT_DN + N_DN
STEPS = DEPTH * PER_LAYER
EARLY = 12


def build(nc, x_in, w_stream, ident_in, rope_in, mask_in, tri_in, conv_in, ln_in, out):
    ctx = ExitStack()
    with ctx:
        def sb(name, shape, dt=F32, stack=ctx):
            return stack.enter_context(nc.sbuf_tensor(name, shape, dt))

        def sem(name):
            return ctx.enter_context(nc.semaphore(name))

        bank = [ctx.enter_context(nc.psum_tensor(f"bank{b}", [P, 512], F32)) for b in range(8)]

        w_raw = [sb(f"w_raw{s}", [P, 2 * UNIT]) for s in range(2)]
        w_hi = [sb(f"w_hi{s}", [P, 2 * UNIT], F32R) for s in range(2)]
        w_lo = [sb(f"w_lo{s}", [P, 2 * UNIT], F32R) for s in range(2)]
        xt_hi = sb("xt_hi", [P, KD, S], F32R)
        xt_lo = sb("xt_lo", [P, KD, S], F32R)
        a_hi = sb("a_hi", [P, KD, S], F32R)
        a_lo = sb("a_lo", [P, KD, S], F32R)
        x = sb("x", [P, NT, D])
        gain = sb("gain", [P, D])
        shift = sb("shift", [P, D])
        ident = sb("ident", [P, P])
        conv = sb("conv", [P, DEPTH * 2 * KF * 4])
        eps = sb("eps", [P, 1])
        stat = sb("stat", [P, NT, 10])

        with ExitStack() as st:
            v_all = sb("v_all", [P, NT, D], stack=st)
            v_pos = [sb(f"v_pos{s}", [P, NT, P], stack=st) for s in range(2)]
            probs_t = [sb(f"probs_t{h}", [P, NT, S], stack=st) for h in range(2)]
            qa = [sb(f"qa{s}", [P, 2, S], stack=st) for s in range(2)]
            ka = [sb(f"ka{s}", [P, S], stack=st) for s in range(2)]
            probs = [sb(f"probs{s}", [P, S], stack=st) for s in range(2)]
            with ExitStack() as ev:
                rope = sb("rope", [P, 2, S], stack=ev)
                masks = sb("masks", [P, 2, S], stack=ev)
                qc = sb("qc", [P, S], stack=ev)
                qs = sb("qs", [P, S], stack=ev)
                kc = sb("kc", [P, S], stack=ev)
                ks = sb("ks", [P, S], stack=ev)
                sm = sb("sm", [P, 2, 4], stack=ev)
            with ExitStack() as od:
                soft = [sb(f"soft{s}", [P, S], stack=od) for s in range(2)]
                tri = sb("tri", [P, P], stack=od)
        with ExitStack() as st:
            h_all = sb("h_all", [P, KF, S], stack=st)
            cg = [sb(f"cg{s}", [P, S], stack=st) for s in range(2)]
            cv = [sb(f"cv{s}", [P, S], stack=st) for s in range(2)]
            sig = [sb(f"sig{s}", [P, S], stack=st) for s in range(2)]
        with ExitStack() as st:
            sb("below_ln", [P, KF, S], stack=st)
            ln_mul = sb("ln_mul", [P, D], stack=st)
            ln_junk = sb("ln_junk", [P, D], stack=st)

        raw_full = [sem(f"raw_full{s}") for s in range(2)]
        first_full = sem("first_full")
        hi_ready = sem("hi_ready")
        lo_ready = sem("lo_ready")
        w_used = sem("w_used")
        x_full = [sem(f"x_full{t}") for t in range(NT)]
        ident_full = sem("ident_full")
        conv_full = sem("conv_full")
        even_full = sem("even_full")
        tri_full = sem("tri_full")
        gb_full = sem("gb_full")
        set_ready = sem("set_ready")
        out_done = sem("out_done")

        def tap(l, tile, k):
            return conv[:, bass.ds((tile + l * 2 * KF) * 4 + k, 1)]

        class Phase:
            def __init__(self, tag, names):
                self.by = {n: sem(f"{tag}_{n}") for n in names.split()}

            def __getitem__(self, n):
                return self.by[n]

        V = [Phase(f"v{l}", "rows act dve") for l in range(DEPTH)]
        both = "q_mm q_ok k_ok s_mm p_ok t_mm tev_a tev_v v_pos pv ot_hi ot_lo "
        A = [Phase("a0", both + "q_cp k_cp q_sw k_sw q_m k_m s_rd ex rc"),
             Phase("a1", both + "zm ab e1 ln sp sc rr")]
        N = [Phase(f"n{i}", "rows sum mean sq lv y0 va nt mulg xn") for i in range(2 * DEPTH)]
        T = [Phase(f"t{i}", "mm hi lo") for i in range(2 * DEPTH)]
        U = [Phase(f"u{l}", "g_mm cg cv g1 gc sg m1 v1 vc h") for l in range(DEPTH)]
        DN = [Phase(f"d{l}", "a_hi a_lo") for l in range(DEPTH)]

        block = ctx.enter_context(nc.Block())

        def filled(c, it):
            return 16 * (c // 2 + it + 1)

        @block.sync
        def _(sp):
            sp.dma_start(w_raw[0][:, 0:UNIT], w_stream[0, :, 0:UNIT]).then_inc(first_full, 16)
            for t in range(NT):
                sp.dma_start(x[:, t, :], x_in[t * P:(t + 1) * P, :]).then_inc(x_full[t], 16)
                if t == 1:
                    sp.dma_start(w_raw[0][:, UNIT:2 * UNIT], w_stream[0, :, UNIT:2 * UNIT])\
                        .then_inc(raw_full[0], 16)
            sp.dma_start(w_raw[1][:, :], w_stream[1]).then_inc(raw_full[1], 16)
            sp.dma_start(rope[:, :, :], rope_in).then_inc(even_full, 16)
            sp.dma_start(masks[:, :, :], mask_in).then_inc(even_full, 16)

            def load(c, it=0):
                sp.wait_ge(lo_ready, 2 * (c + 2 * it) - 2)
                sp.dma_start(w_raw[c % 2][:, :], w_stream[c + 2 * it]).then_inc(raw_full[c % 2], 16)

            def swap(dst, src, copied, swapped, i):
                sp.wait_ge(copied, i + 1)
                for n in range(2):
                    sp.dma_start(dst[n::2, :], src[1 - n::2, :]).then_inc(swapped, 16)

            def swaps(i):
                swap(qs, qc, A[0]["q_cp"], A[0]["q_sw"], i)
                swap(ks, kc, A[0]["k_cp"], A[0]["k_sw"], i)

            ahead = AT_QK + 3
            for c in range(2, ahead):
                load(c)
                if c == 2:
                    swaps(0)
            with sp.Fori(0, 3) as it:
                for j in range(2):
                    load(ahead + j, it)
                    swaps(2 * it + j + 1)
            load(ahead + 6)
            swaps(7)
            with sp.Fori(0, (STEPS - ahead - 7) // 2) as it:
                for j in range(2):
                    load(ahead + 7 + j, it)
            for t in range(NT):
                sp.wait_ge(N[-1]["xn"], t + 1)
                sp.dma_start(out[t * P:(t + 1) * P, :], x[:, t, :]).then_inc(out_done, 16)
            sp.wait_ge(out_done, 16 * NT)

        @block.gpsimd
        def _(pool):
            def rest(c, it=0):
                s = c % 2
                for u in range(2):
                    pool.wait_ge(hi_ready, 2 * (c + 2 * it) + u + 1)
                    part = slice(u * UNIT, (u + 1) * UNIT)
                    pool.tensor_tensor(w_lo[s][:, part], w_raw[s][:, part],
                                       w_hi[s][:, part].bitcast(F32), ALU.subtract).then_inc(lo_ready, 1)

            def rotate_q(slot, i):
                a = A[0]
                pool.wait_ge(a["q_sw"], 32 * (i + 1))
                for n, (t, tab) in enumerate(((qc, 0), (qs, 1))):
                    pool.tensor_tensor(t[:, :], t[:, :], rope[:, tab, :], ALU.mult).then_inc(a["q_m"], 1)
                pool.wait_ge(a["q_m"], 2 * i + 2)
                for h in range(2):
                    part = slice(64 * h, 64 * h + 64)
                    pool.tensor_tensor(qa[slot][part, h, :], qc[part, :], qs[part, :],
                                       ALU.add).then_inc(a["q_ok"], 1)
                    pool.wait_ge(a["q_ok"], 2 * i + h + 1)

            for l in range(DEPTH):
                b = l * PER_LAYER
                for c in range(AT_QK + 2):
                    rest(b + c)
                    if l == 0 and c == 1:
                        pool.wait_ge(even_full, 32)
                        rotate_q(0, 0)
                for sname in ("act", "dve"):
                    pool.wait_ge(V[l][sname], NT)

                def position(j, it, dense):
                    pool.wait_ge(w_used, b + AT_QK + 2 * it + j + 1)
                    pool.tensor_copy(v_pos[j % 2][:, :, :], v_all[:, :, bass.ds((2 * it + j) * P, P)])\
                        .then_inc(A[l]["v_pos"], 1)
                    rest(b + AT_QK + 2 + j, it)
                    if l == 0 and dense:
                        rotate_q((j + 1) % 2, 2 * it + j + 1)

                with pool.Fori(0, 3) as it:
                    position(0, it, True)
                    position(1, it, True)
                position(6, 0, True)
                position(7, 0, False)
                rest(b + AT_O + 2)
                rest(b + AT_O + 3)
                with pool.Fori(0, (PER_LAYER - AT_UP) // 2) as it:
                    for j in range(2):
                        rest(b + AT_UP + j, it)
                if (PER_LAYER - AT_UP) % 2:
                    rest(b + PER_LAYER - 1)

        @block.scalar
        def _(act):
            def heads(c, it=0, used=True):
                act.wait_ge(raw_full[c % 2], filled(c, it))
                if used:
                    act.wait_ge(w_used, c + 2 * it - 1)
                act.activation(w_hi[c % 2][:, :], w_raw[c % 2][:, :], ACT.Copy).then_inc(hi_ready, 2)

            def unit_heads(c, u):
                act.wait_ge(raw_full[c % 2], filled(c, 0))
                act.wait_ge(w_used, c - 1)
                part = slice(u * UNIT, (u + 1) * UNIT)
                act.activation(w_hi[c % 2][:, part], w_raw[c % 2][:, part], ACT.Copy).then_inc(hi_ready, 1)

            def load_gain(i):
                for row, dst in ((0, gain), (1, shift)):
                    act.dma_start(dst[:, :], ln_in[i, row:row + 1, :].broadcast_to([P, D])).then_inc(gb_full, 16)

            def xt_heads(i, t):
                act.wait_ge(T[i]["mm"], t + 1)
                for g in range(2):
                    act.activation(xt_hi[:, 4 * g:4 * g + 4, t * P:(t + 1) * P],
                                   bank[2 * t + g][:, :].rearrange("p (k q) -> p k q", k=4),
                                   ACT.Copy).then_inc(T[i]["hi"], 1)

            def norm_stats(i, t):
                n = N[i]
                act.wait_ge(n["mean"], t + 1)
                act.activation(ln_junk[:, :], x[:, t, :], ACT.Square, bias=stat[:, t, 2:3],
                               accum_out=stat[:, t, 3:4]).then_inc(n["sq"], 1)
                act.wait_ge(n["sq"], t + 1)
                act.activation(stat[:, t, 4:5], stat[:, t, 3:4], ACT.Ln, bias=eps[:, 0:1],
                               scale=1.0 / D).then_inc(n["lv"], 1)
                act.wait_ge(n["lv"], t + 1)
                act.activation(stat[:, t, 5:6], stat[:, t, 4:5], ACT.Exp, scale=-0.5).then_inc(n["y0"], 1)

            def values(l):
                for t in range(NT):
                    if t < NT - 1:
                        act.wait_ge(V[l]["rows"], t + 1)
                    else:
                        act.wait_ge(w_used, l * PER_LAYER + AT_QK + 1)
                    act.activation(v_all[:, t, 0:HALF], bank[2 * t][:, :], ACT.Copy).then_inc(V[l]["act"], 1)

            def turn_out(a, j, g):
                act.wait_ge(a["t_mm"], g + 1)
                qi = j % NT
                act.activation(probs_t[j // NT][:, 0:qi + 1, qi * P:(qi + 1) * P],
                               bank[4 + j % 2][:, 0:(qi + 1) * P].rearrange("p (k q) -> p k q", q=P),
                               ACT.Copy).then_inc(a["tev_a"], 1)

            def out_heads(a, i, slot):
                act.wait_ge(a["pv"], i + 1)
                act.activation(a_hi[:, bass.ds(i, 1), :],
                               bank[6 + slot][:, :].rearrange("p (a q) -> p a q", a=1),
                               ACT.Copy).then_inc(a["ot_hi"], 1)

            def even_body(b, c, it, dense, before):
                a = A[0]
                i = c + 2 * it
                for j in range(8):
                    g = 8 * i + j
                    if j == 2:
                        if before:
                            out_heads(a, i - 1, (c - 1) % 2)
                        heads(b + AT_QK + c + 2, it)
                    if j % 2 == 1 and j >= 3:
                        turn_out(a, j - 2, g - 2)
                    if j == 4 and dense:
                        act.wait_ge(a["q_mm"], i + 2)
                        act.activation(qc[:, :], bank[0][:, :], ACT.Copy, scale=-MOBA_SCALE).then_inc(a["q_cp"], 1)
                    if j == 7 and dense:
                        act.wait_ge(w_used, b + AT_QK + i + 2)
                        act.activation(kc[:, :], bank[1][:, :], ACT.Copy).then_inc(a["k_cp"], 1)
                    act.wait_ge(a["s_rd"], g + 1)
                    L = (j % NT + 1) * P
                    act.activation(probs[j % 2][:, 0:L], probs[j % 2][:, 0:L], ACT.Exp,
                                   bias=sm[:, j % 2, 0:1], scale=-1.0,
                                   accum_out=sm[:, j % 2, 1:2]).then_inc(a["ex"], 1)
                turn_out(a, 7, 8 * i + 7)

            def odd_body(b, c, it, dense, before):
                a = A[1]
                i = c + 2 * it

                def soft_part(j):
                    g, L = 4 * i + j, (j + 1) * P
                    e = soft[j % 2][:, 0:L]
                    act.wait_ge(a["zm"], g + 1)
                    act.activation(e, bank[2 + j % 2][:, 0:L], ACT.Abs).then_inc(a["ab"], 1)
                    act.wait_ge(a["ab"], g + 1)
                    act.activation(e, e, ACT.Exp, scale=-1.0).then_inc(a["e1"], 1)
                    act.wait_ge(a["e1"], g + 1)
                    act.activation(e, e, ACT.Ln, bias=1.0).then_inc(a["ln"], 1)

                def weight_part(j):
                    g, L = 4 * i + j, (j + 1) * P
                    act.wait_ge(a["rr"], g + 1)
                    act.activation(probs[j % 2][:, 0:L], probs[j % 2][:, 0:L], ACT.Exp).then_inc(a["p_ok"], 1)

                for j in range(4):
                    if j == 2 and before:
                        out_heads(a, i - 1, (c - 1) % 2)
                    if j == 0:
                        heads(b + AT_QK + c + 2, it)
                    if j == 3:
                        turn_out(a, 1, 4 * i + 1)
                        if dense:
                            act.wait_ge(a["q_mm"], i + 2)
                            act.activation(qa[(c + 1) % 2][:, 0, :], bank[0][:, :], ACT.Copy,
                                           scale=SB_SCALE).then_inc(a["q_ok"], 1)
                    if j == 2:
                        weight_part(1)
                    soft_part(j)
                    if j % 2:
                        weight_part(j - 1)
                weight_part(3)
                turn_out(a, 3, 4 * i + 3)
                if dense:
                    act.wait_ge(w_used, b + AT_QK + i + 2)
                    act.activation(ka[(c + 1) % 2][:, :], bank[1][:, :], ACT.Copy).then_inc(a["k_ok"], 1)

            act.dma_start(ident[:, :], ident_in).then_inc(ident_full, 16)
            act.preload_act_table_set("natural_log_exp_and_others")
            act.wait_ge(first_full, 16)
            act.activation(w_hi[0][:, 0:UNIT], w_raw[0][:, 0:UNIT], ACT.Copy).then_inc(hi_ready, 1)
            act.wait_ge(set_ready, 5)
            xt_heads(0, 0)
            xt_heads(0, 1)
            act.wait_ge(raw_full[0], 16)
            act.activation(w_hi[0][:, UNIT:2 * UNIT], w_raw[0][:, UNIT:2 * UNIT], ACT.Copy)\
                .then_inc(hi_ready, 1)
            xt_heads(0, 2)
            xt_heads(0, 3)
            heads(1, used=False)
            act.dma_start(conv[:, :], conv_in).then_inc(conv_full, 16)
            load_gain(0)

            for l in range(DEPTH):
                b = l * PER_LAYER
                if l == 0:
                    a = A[0]
                    act.wait_ge(a["q_mm"], 1)
                    act.activation(qc[:, :], bank[0][:, :], ACT.Copy, scale=-MOBA_SCALE).then_inc(a["q_cp"], 1)
                    act.wait_ge(w_used, b + 1)
                    act.activation(kc[:, :], bank[1][:, :], ACT.Copy).then_inc(a["k_cp"], 1)
                    body = even_body
                else:
                    a = A[1]
                    act.wait_ge(N[1]["xn"], NT)
                    act.dma_start(tri[:, :], tri_in).then_inc(tri_full, 16)
                    act.wait_ge(a["q_mm"], 1)
                    act.activation(qa[0][:, 0, :], bank[0][:, :], ACT.Copy, scale=SB_SCALE).then_inc(a["q_ok"], 1)
                    act.wait_ge(w_used, b + 1)
                    act.activation(ka[0][:, :], bank[1][:, :], ACT.Copy).then_inc(a["k_ok"], 1)
                    body = odd_body
                for c in range(2, AT_QK + 2):
                    heads(b + c)
                values(l)
                body(b, 0, 0, True, False)
                with act.Fori(0, 3) as it:
                    body(b, 1, it, True, True)
                    body(b, 2, it, True, True)
                body(b, 7, 0, False, True)
                out_heads(A[l], 7, 1)
                for c in range(2):
                    heads(b + AT_O + 2 + c)
                for i, after in ((2 * l, b + AT_O + 4), (2 * l + 1, b + PER_LAYER)):
                    if i % 2:
                        def chunk_heads(c, it=0, used=True):
                            j = c + 2 * it
                            act.wait_ge(U[l]["h"], 2 * j + 2)
                            if used:
                                act.wait_ge(w_used, b + AT_DN + j - 1)
                            act.activation(a_hi[:, 2 * (c % 2):2 * (c % 2) + 2, :],
                                           h_all[:, bass.ds(2 * j, 2), :], ACT.Copy).then_inc(DN[l]["a_hi"], 1)

                        def up_body(c, it, first):
                            f, u = c + 2 * it, U[l]
                            s = c % 2
                            act.wait_ge(u["g_mm"], f + 1)
                            if not first:
                                act.wait_ge(u["h"], f - 1)
                            act.activation(cg[s][:, :], bank[2 * s][:, :], ACT.Identity,
                                           bias=tap(l, f, 3),
                                           scale=tap(l, f, 2)).then_inc(u["cg"], 1)
                            act.wait_ge(u["gc"], f + 1)
                            act.activation(sig[s][:, :], cg[s][:, :], ACT.Sigmoid).then_inc(u["sg"], 1)
                            act.wait_ge(w_used, b + AT_UP + f + 1)
                            act.activation(cv[s][:, :], bank[2 * s + 1][:, :], ACT.Identity,
                                           bias=tap(l, f + KF, 3),
                                           scale=tap(l, f + KF, 2)).then_inc(u["cv"], 1)
                            heads(b + AT_UP + c + 2, it)

                        act.preload_act_table(ACT.Sigmoid)
                        act.wait_ge(conv_full, 16)
                        up_body(0, 0, True)
                        up_body(1, 0, True)
                        chunk_heads(0, used=False)
                        with act.Fori(1, KF // 2) as it:
                            up_body(0, it, False)
                            up_body(1, it, False)

                        act.preload_act_table_set("natural_log_exp_and_others")
                        chunk_heads(1)
                        chunk_heads(2)
                        heads(b + AT_DN + 2)
                        with act.Fori(0, 4) as it:
                            for j in (1, 2):
                                heads(b + AT_DN + 2 + j, it)
                                chunk_heads(j + 2, it)
                    if i == 2 * DEPTH - 1:
                        for t in range(NT):
                            norm_stats(i, t)
                    else:
                        norm_stats(i, 0)
                        norm_stats(i, 1)
                        xt_heads(i + 1, 0)
                        norm_stats(i, 2)
                        unit_heads(after, 0)
                        xt_heads(i + 1, 1)
                        unit_heads(after, 1)
                        heads(after + 1)
                        norm_stats(i, 3)
                        xt_heads(i + 1, 2)
                        xt_heads(i + 1, 3)
                        act.wait_ge(N[i]["xn"], NT)
                        load_gain(i + 1)

        @block.vector
        def _(dve):
            def xt_rests(i, t):
                dve.wait_ge(T[i]["hi"], 2 * t + 2)
                for g in range(2):
                    part = xt_hi[:, 4 * g:4 * g + 4, t * P:(t + 1) * P]
                    dve.tensor_tensor(xt_lo[:, 4 * g:4 * g + 4, t * P:(t + 1) * P],
                                      bank[2 * t + g][:, :].rearrange("p (k q) -> p k q", k=4),
                                      part.bitcast(F32), ALU.subtract).then_inc(T[i]["lo"], 1)

            def norm_sum(i, t):
                n = N[i]
                if t < NT - 1:
                    dve.wait_ge(n["rows"], t + 1)
                else:
                    dve.wait_ge(w_used, i // 2 * PER_LAYER + (PER_LAYER if i % 2 else AT_UP))
                for g in range(2):
                    dve.scalar_tensor_tensor(out=x[:, t, g * HALF:(g + 1) * HALF],
                                             in0=x[:, t, g * HALF:(g + 1) * HALF], scalar=ALPHA,
                                             in1=bank[2 * t + g][:, :], op0=ALU.mult, op1=ALU.add,
                                             accum_out=stat[:, t, g:g + 1]).then_inc(n["sum"], 1)
                dve.wait_ge(n["sum"], 2 * t + 2)
                dve.tensor_scalar(stat[:, t, 2:3], stat[:, t, 0:1], stat[:, t, 1:2], -1.0 / D,
                                  ALU.add, ALU.mult).then_inc(n["mean"], 1)

            def norm_mul(i, t):
                n = N[i]
                dve.wait_ge(n["mean"], t + 1)
                if t == 0:
                    dve.wait_ge(gb_full, 32 * (i + 1))
                else:
                    dve.wait_ge(n["xn"], t)
                dve.scalar_tensor_tensor(out=ln_mul[:, :], in0=x[:, t, :], scalar=stat[:, t, 2:3],
                                         in1=gain[:, :], op0=ALU.add, op1=ALU.mult).then_inc(n["mulg"], 1)

            def norm_out(i, t):
                n = N[i]
                v, y0, w, r = (stat[:, t, k:k + 1] for k in (6, 5, 7, 8))
                dve.wait_ge(n["sq"], t + 1)
                dve.tensor_scalar(v, stat[:, t, 3:4], 1.0 / D, EPS, ALU.mult, ALU.add).then_inc(n["va"], 1)
                dve.wait_ge(n["va"], t + 1)
                dve.wait_ge(n["y0"], t + 1)
                dve.scalar_tensor_tensor(out=w, in0=y0, scalar=v, in1=y0, op0=ALU.mult,
                                         op1=ALU.mult).then_inc(n["nt"], 1)
                dve.wait_ge(n["nt"], 3 * t + 1)
                dve.tensor_scalar(w, w, -0.5, 1.5, ALU.mult, ALU.add).then_inc(n["nt"], 1)
                dve.wait_ge(n["nt"], 3 * t + 2)
                dve.tensor_tensor(r, y0, w, ALU.mult).then_inc(n["nt"], 1)
                dve.wait_ge(n["nt"], 3 * t + 3)
                dve.wait_ge(n["mulg"], t + 1)
                dve.scalar_tensor_tensor(out=x[:, t, :], in0=ln_mul[:, :], scalar=r, in1=shift[:, :],
                                         op0=ALU.mult, op1=ALU.add).then_inc(n["xn"], 1)

            def norm(i):
                turn = i < 2 * DEPTH - 1
                norm_sum(i, 0)
                norm_mul(i, 0)
                norm_sum(i, 1)
                norm_out(i, 0)
                norm_mul(i, 1)
                norm_out(i, 1)
                norm_sum(i, 2)
                norm_mul(i, 2)
                if turn:
                    xt_rests(i + 1, 0)
                    norm_out(i, 2)
                    xt_rests(i + 1, 1)
                    norm_sum(i, 3)
                    norm_mul(i, 3)
                    norm_out(i, 3)
                    xt_rests(i + 1, 2)
                    xt_rests(i + 1, 3)
                else:
                    norm_sum(i, 3)
                    norm_out(i, 2)
                    norm_mul(i, 3)
                    norm_out(i, 3)

            def rope_k_cos(a, s, i):
                dve.wait_ge(a["k_cp"], i + 1)
                dve.tensor_tensor(ka[s][:, :], kc[:, :], rope[:, 0, :], ALU.mult).then_inc(a["k_m"], 1)

            def rope_k_sin(a, s, i):
                dve.wait_ge(a["k_sw"], 32 * (i + 1))
                dve.tensor_tensor(ks[:, :], ks[:, :], rope[:, 1, :], ALU.mult).then_inc(a["k_m"], 1)
                dve.wait_ge(a["k_m"], 2 * i + 2)
                dve.tensor_tensor(ka[s][:, :], ka[s][:, :], ks[:, :], ALU.add).then_inc(a["k_ok"], 1)

            def turn_out(a, j, g):
                dve.wait_ge(a["t_mm"], g + 1)
                qi = j % NT
                dve.tensor_copy(probs_t[j // NT][:, 0:qi + 1, qi * P:(qi + 1) * P],
                                bank[4 + j % 2][:, 0:(qi + 1) * P].rearrange("p (k q) -> p k q", q=P))\
                    .then_inc(a["tev_v"], 1)

            def out_rests(a, i, par):
                dve.wait_ge(a["ot_hi"], i + 1)
                dve.tensor_tensor(a_lo[:, bass.ds(i, 1), :],
                                  bank[6 + par][:, :].rearrange("p (a q) -> p a q", a=1),
                                  a_hi[:, bass.ds(i, 1), :].bitcast(F32), ALU.subtract).then_inc(a["ot_lo"], 1)

            def even_body(c, it, dense, before, kind):
                a, i = A[0], c + 2 * it

                def bound(j):
                    g, qi = 8 * i + j, j % NT
                    L = (qi + 1) * P
                    dve.wait_ge(a["s_mm"], g + 1)
                    dve.memset(sm[:, j % 2, 3:4], 0.0)
                    dve.tensor_tensor_reduce(probs[j % 2][:, 0:L], bank[2 + j % 2][:, 0:L],
                                             masks[:, kind, S - L:S], 1.0, 3e38, ALU.add, ALU.min,
                                             sm[:, j % 2, 0:1]).then_inc(a["s_rd"], 1)

                def divide(j):
                    g, L = 8 * i + j, (j % NT + 1) * P
                    dve.wait_ge(a["ex"], g + 1)
                    dve.reciprocal(sm[:, j % 2, 2:3], sm[:, j % 2, 1:2]).then_inc(a["rc"], 1)
                    dve.wait_ge(a["rc"], g + 1)
                    dve.tensor_scalar(probs[j % 2][:, 0:L], probs[j % 2][:, 0:L], sm[:, j % 2, 2:3], None,
                                      ALU.mult).then_inc(a["p_ok"], 1)

                for j in range(8):
                    if j >= 2 and j % 2 == 0:
                        turn_out(a, j - 2, 8 * i + j - 2)
                    if j >= 2:
                        divide(j - 1)
                    bound(j)
                    if j == 1:
                        divide(0)
                    if j == 2 and before:
                        out_rests(a, i - 1, (c - 1) % 2)
                if dense:
                    rope_k_cos(a, (c + 1) % 2, i + 1)
                divide(7)
                turn_out(a, 6, 8 * i + 6)
                if dense:
                    rope_k_sin(a, (c + 1) % 2, i + 1)

            def odd_body(c, it, dense, before, kind):
                a, i = A[1], c + 2 * it

                def mask_diagonal(j):
                    dve.wait_ge(a["s_mm"], 4 * i + j + 1)
                    z = bank[2 + j % 2][:, j * P:(j + 1) * P]
                    dve.tensor_tensor(z, z, tri[:, :], ALU.add).then_inc(a["zm"], 1)

                def break_stick(j):
                    g, L = 4 * i + j, (j + 1) * P
                    z, e, r = bank[2 + j % 2][:, 0:L], soft[j % 2], probs[j % 2]
                    dve.wait_ge(a["ln"], g + 1)
                    dve.scalar_tensor_tensor(out=e[:, 0:L], in0=z, scalar=0.0, in1=e[:, 0:L],
                                             op0=ALU.max, op1=ALU.add).then_inc(a["sp"], 1)
                    dve.wait_ge(a["sp"], g + 1)
                    back = e[:, L - 1::-1]
                    dve.tensor_tensor_scan(r[:, L - 1::-1], back, back, 0.0, ALU.add,
                                           ALU.max).then_inc(a["sc"], 1)
                    dve.wait_ge(a["sc"], g + 1)
                    dve.tensor_tensor(r[:, 0:L], z, r[:, 0:L], ALU.subtract).then_inc(a["rr"], 1)

                for j in range(4):
                    if j == 2:
                        turn_out(a, 0, 4 * i)
                    if j == 2:
                        break_stick(1)
                    mask_diagonal(j)
                    if j % 2:
                        break_stick(j - 1)
                    if j == 2 and before:
                        out_rests(a, i - 1, (c - 1) % 2)
                break_stick(3)
                turn_out(a, 2, 4 * i + 2)

            dve.memset(eps[:, :], EPS).then_inc(set_ready, 1)
            for s in range(2):
                dve.memset(qa[s][P // 2:P, 0, :], 0.0).then_inc(set_ready, 1)
                dve.memset(qa[s][0:P // 2, 1, :], 0.0).then_inc(set_ready, 1)
            dve.wait_ge(set_ready, 5)
            for t in range(NT):
                xt_rests(0, t)
            for l in range(DEPTH):
                if l == 0:
                    a = A[0]
                    dve.wait_ge(even_full, 32)
                    rope_k_cos(a, 0, 0)
                    rope_k_sin(a, 0, 0)
                    body = even_body
                else:
                    dve.wait_ge(tri_full, 16)
                    body = odd_body
                for t in range(NT):
                    if t < NT - 1:
                        dve.wait_ge(V[l]["rows"], t + 1)
                    else:
                        dve.wait_ge(w_used, l * PER_LAYER + AT_QK + 1)
                    dve.tensor_copy(v_all[:, t, HALF:D], bank[2 * t + 1][:, :]).then_inc(V[l]["dve"], 1)
                body(0, 0, True, False, 1)
                with dve.Fori(0, 3) as it:
                    body(1, it, True, True, 0)
                    body(2, it, True, True, 0)
                body(7, 0, False, True, 1)
                out_rests(A[l], 7, 1)
                norm(2 * l)

                def up_body(c, it):
                    f, u, s = c + 2 * it, U[l], c % 2

                    def convolve(ps, acc, tile, start, mid, end):
                        dve.wait_ge(start, f + 1)
                        dve.scalar_tensor_tensor(out=acc[:, 1:S], in0=ps[:, 0:S - 1],
                                                 scalar=tap(l, tile, 1), in1=acc[:, 1:S],
                                                 op0=ALU.mult, op1=ALU.add).then_inc(mid, 1)
                        dve.wait_ge(mid, f + 1)
                        dve.scalar_tensor_tensor(out=acc[:, 2:S], in0=ps[:, 0:S - 2],
                                                 scalar=tap(l, tile, 0), in1=acc[:, 2:S],
                                                 op0=ALU.mult, op1=ALU.add).then_inc(end, 1)

                    convolve(bank[2 * s], cg[s], f, u["cg"], u["g1"], u["gc"])
                    dve.wait_ge(u["sg"], f + 1)
                    dve.tensor_tensor(sig[s][:, :], sig[s][:, :], cg[s][:, :], ALU.mult).then_inc(u["m1"], 1)
                    convolve(bank[2 * s + 1], cv[s], f + KF, u["cv"], u["v1"], u["vc"])
                    dve.wait_ge(u["vc"], f + 1)
                    dve.wait_ge(u["m1"], f + 1)
                    dve.tensor_tensor(h_all[:, bass.ds(f, 1), :],
                                      sig[s][:, :].rearrange("p (a q) -> p a q", a=1),
                                      cv[s][:, :].rearrange("p (a q) -> p a q", a=1), ALU.mult).then_inc(u["h"], 1)

                def chunk_rests(c, it=0):
                    j = c + 2 * it
                    dve.wait_ge(DN[l]["a_hi"], j + 1)
                    k = 2 * (c % 2)
                    dve.tensor_tensor(a_lo[:, k:k + 2, :], h_all[:, bass.ds(2 * j, 2), :],
                                      a_hi[:, k:k + 2, :].bitcast(F32), ALU.subtract).then_inc(DN[l]["a_lo"], 1)

                dve.wait_ge(conv_full, 16)
                up_body(0, 0)
                up_body(1, 0)
                chunk_rests(0)
                with dve.Fori(1, KF // 2) as it:
                    up_body(0, it)
                    up_body(1, it)
                with dve.Fori(0, N_DN // 2) as it:
                    chunk_rests(1, it)
                    chunk_rests(2, it)
                norm(2 * l + 1)

        @block.tensor
        def _(pe):
            def turn_x(i, t):
                if i == 0:
                    pe.wait_ge(x_full[t], 16)
                else:
                    pe.wait_ge(N[i - 1]["xn"], t + 1)
                for k in range(KD):
                    mm = pe.transpose(bank[2 * t + k // 4][:, (k % 4) * P:(k % 4 + 1) * P],
                                      x[:, t, k * P:(k + 1) * P], ident[:, :])
                mm.then_inc(T[i]["mm"], 1)

            def row_tiles(steps, a, first_chunk, last, rows, visits, before=None, partial=False):
                for v, (t, m) in enumerate(visits):
                    if before:
                        before(t, m)
                    c, it, slot = steps[m]
                    s = c % 2
                    opens = m not in [n for _, n in visits[:v]]
                    frees = m not in [n for _, n in visits[v + 1:]] and not partial
                    for u in range(2):
                        if opens:
                            pe.wait_ge(lo_ready, 2 * (c + 2 * it) + u + 1)
                        hi = a[0][:, slot + u, t * P:(t + 1) * P]
                        lo = a[1][:, slot + u, t * P:(t + 1) * P]
                        first = first_chunk and m == 0 and u == 0
                        end = last and m == len(steps) - 1 and u == 1
                        for n, (lhs, w) in enumerate(((hi, w_hi), (hi, w_lo), (lo, w_hi))):
                            for g in range(2):
                                mm = pe.matmul(bank[2 * t + g][:, :], lhs,
                                               w[s][:, u * UNIT + g * HALF:u * UNIT + (g + 1) * HALF],
                                               start=first and n == 0, stop=end and n == 2)
                                if (u, n, g) == (1, 2, 1):
                                    if frees:
                                        mm.then_inc(w_used, 1)
                                    elif end:
                                        mm.then_inc(rows, 1)
                                yield mm

            one_step = [(t, 0) for t in range(NT)]
            last_two = [(0, 0), (1, 0), (0, 1), (1, 1), (2, 0), (2, 1), (3, 0), (3, 1)]

            def row_steps(*args, **kw):
                for _ in row_tiles(*args, **kw):
                    pass

            def col_unit(c, it, u, out_bank, tile_done, half=None, part=slice(None)):
                s = c % 2
                tok = slice(0, S) if half is None else slice(half * S // 2, (half + 1) * S // 2)
                todo = []
                for k in range(KD):
                    at = slice(u * UNIT + k * P, u * UNIT + (k + 1) * P)
                    todo += [(w_hi[s][:, at], xt_hi[:, k, tok]), (w_hi[s][:, at], xt_lo[:, k, tok]),
                             (w_lo[s][:, at], xt_hi[:, k, tok])]
                for n, (w, m) in list(enumerate(todo))[part]:
                    if n == 0:
                        pe.wait_ge(lo_ready, 2 * (c + 2 * it) + u + 1)
                    mm = pe.matmul(out_bank[:, tok], w, m, start=n == 0, stop=n == len(todo) - 1)
                    if n == len(todo) - 1 and half != 0:
                        mm.then_inc(w_used if u else tile_done, 1)
                    yield mm

            def first_columns(c, bank0, signal, i, meanwhile):
                for half in range(2):
                    pe.wait_ge(T[i]["lo"], NT * (half + 1))
                    for unit in range(2):
                        for _ in col_unit(c, 0, unit, bank[bank0 + unit], signal, half):
                            pass
                    if half == 0 and i > 0:
                        turn_x(i, 3)
                        meanwhile()

            def project_early(a, l, b, c, it):
                pe.wait_ge(a["q_ok" if l else "q_cp"], c + 2 * it)
                yield from col_unit(b + AT_QK + c, it, 0, bank[0], None, part=slice(0, EARLY))

            def project(a, b, c, it):
                yield from col_unit(b + AT_QK + c, it, 0, bank[0], a["q_mm"], part=slice(EARLY, None))
                yield from col_unit(b + AT_QK + c, it, 1, bank[1], None)

            def position(l, b, c, it, dense, early=False, filler=None):
                a, i = A[l], c + 2 * it
                par = c % 2
                steps = 8 if l == 0 else 4
                heads = 2 if l == 0 else 1
                more = project(a, b, c + 1, it) if dense else filler
                if early:
                    more = chain(more, project_early(a, l, b, c + 2, it))
                if dense:
                    share = (7, 6, 6, 6, 6, 5, 2, 3, 3) if l == 0 else (10, 11, 14, 9, 2)
                else:
                    share = (3,) * 8 + (0,) if l == 0 else (6,) * 4 + (0,)

                def fill(n):
                    for _ in range(n):
                        next(more, None)

                def scores(j):
                    h, qi = j // NT, j % NT
                    pe.matmul(bank[2 + j % 2][:, 0:(qi + 1) * P], qa[par][:, h, qi * P:(qi + 1) * P],
                              ka[par][:, 0:(qi + 1) * P], start=True, stop=True).then_inc(a["s_mm"], 1)

                def turn(j):
                    g, qi = steps * i + j, j % NT
                    pe.wait_ge(a["p_ok"], g + 1)
                    if j >= 2:
                        ev, n = (a["tev_v"], j // 2) if j % 2 == 0 else (a["tev_a"], j // 2)
                        pe.wait_ge(ev, steps // 2 * i + n)
                    for kj in range(qi + 1):
                        mm = pe.transpose(bank[4 + j % 2][:, kj * P:(kj + 1) * P],
                                          probs[j % 2][:, kj * P:(kj + 1) * P], ident[:, :])
                    mm.then_inc(a["t_mm"], 1)

                def weigh(h, *tiles):
                    if (h, tiles[0]) == (0, 0):
                        pe.wait_ge(a["v_pos"], i + 1)
                    dh = P // heads
                    for qi in tiles:
                        pe.wait_ge(a["tev_a"] if qi % 2 else a["tev_v"],
                                   steps // 2 * i + (h * NT + qi) // 2 + 1)
                        for kj in range(qi + 1):
                            mm = pe.matmul(bank[6 + par][h * dh:(h + 1) * dh, qi * P:(qi + 1) * P],
                                           v_pos[par][:, kj, h * dh:(h + 1) * dh],
                                           probs_t[h][:, kj, qi * P:(qi + 1) * P],
                                           start=kj == 0, stop=kj == qi)
                    if (h, qi) == (heads - 1, NT - 1):
                        mm.then_inc(a["pv"], 1)

                pe.wait_ge(a["q_ok"], heads * (i + 1))
                pe.wait_ge(a["k_ok"], i + 1)
                scores(0)
                scores(1)
                for j in range(steps):
                    fill(share[j])
                    if l == 0 and j == 5:
                        weigh(0, 0, 1)
                    if l == 0 and j == 6:
                        weigh(0, 2, 3)
                    if l == 0 and j == 7:
                        weigh(1, 0)
                    if l == 1 and j == 3:
                        weigh(0, 0, 1)
                    turn(j)
                    if j + 2 < steps:
                        scores(j + 2)
                if l == 0:
                    weigh(1, 1)
                weigh(heads - 1, 2)
                fill(share[steps])
                weigh(heads - 1, 3)
                for _ in more:
                    pass

            pe.wait_ge(ident_full, 16)
            for t in range(NT):
                turn_x(0, t)
            for l in range(DEPTH):
                b = l * PER_LAYER
                def turning(i):
                    def before(t, n):
                        if t == NT - 1:
                            turn_x(i, n)
                    return before

                def first_v(t, _):
                    if t == 0:
                        if l == 0:
                            pe.wait_ge(A[l]["q_cp"], 1)
                            pe.wait_ge(A[l]["k_cp"], 1)
                        else:
                            pe.wait_ge(A[l]["q_ok"], 1)
                            pe.wait_ge(A[l]["k_ok"], 1)

                v_first = row_tiles([(b + AT_V, 0, 0)], (xt_hi, xt_lo), True, False, None,
                                    one_step[1:] + one_step[:1], first_v)

                def v_meanwhile():
                    for _ in range(12):
                        next(v_first)

                first_columns(b, 0, A[l]["q_mm"], 2 * l, v_meanwhile)
                for _ in v_first:
                    pass
                for c in range(1, N_V):
                    row_steps([(b + AT_V + c, 0, 2 * c)], (xt_hi, xt_lo), False, c == N_V - 1, V[l]["rows"],
                              one_step)
                pe.wait_ge(V[l]["act"], NT)
                pe.wait_ge(V[l]["dve"], NT)
                for _ in project_early(A[l], l, b, 1, 0):
                    pass
                position(l, b, 0, 0, True, True)
                with pe.Fori(0, 2) as it:
                    position(l, b, 1, it, True, True)
                    position(l, b, 2, it, True, True)
                position(l, b, 5, 0, True, True)
                position(l, b, 6, 0, True)
                out_steps = [(b + AT_O + c, 0, 2 * c) for c in range(N_O)]
                position(l, b, 7, 0, False, filler=row_tiles(out_steps[:2], (a_hi, a_lo), True, False,
                                                             None, [(0, 0), (0, 1)], partial=True))
                pe.wait_ge(A[l]["ot_lo"], 2 * 2)

                def last_output(t, _):
                    if t == 3:
                        pe.wait_ge(A[l]["ot_lo"], NPOS)
                row_steps(out_steps[:2], (a_hi, a_lo), True, False, None,
                          [(t, n) for n in range(2) for t in (1, 2, 3)], last_output)
                row_steps(out_steps[2:], (a_hi, a_lo), False, True, N[2 * l]["rows"], last_two,
                          turning(2 * l + 1))
                turn_x(2 * l + 1, 2)

                def up_body(c, it):
                    f, u, s = c + 2 * it, U[l], c % 2
                    pe.wait_ge(u["gc"], f - 1)
                    for _ in col_unit(b + AT_UP + c, it, 0, bank[2 * s], u["g_mm"]):
                        pass
                    pe.wait_ge(u["vc"], f - 1)
                    for _ in col_unit(b + AT_UP + c, it, 1, bank[2 * s + 1], None):
                        pass

                def up_half(half):
                    for unit in range(2):
                        for _ in col_unit(b + AT_UP + 1, 0, unit, bank[2 + unit], U[l]["g_mm"], half):
                            pass

                first_columns(b + AT_UP, 0, U[l]["g_mm"], 2 * l + 1, lambda: up_half(0))
                up_half(1)
                with pe.Fori(1, KF // 2) as it:
                    up_body(0, it)
                    up_body(1, it)

                def down(pairs, first, last):
                    steps = [(b + AT_DN + c, it, 2 * (c % 2)) for c, it in pairs]

                    turn = turning(2 * l + 2) if last and l < DEPTH - 1 else None

                    def chunk(t, n):
                        if turn:
                            turn(t, n)
                        if first and t == 0:
                            pe.wait_ge(U[l]["vc"], KF - 1)
                        if first and t == 1:
                            pe.wait_ge(U[l]["vc"], KF)
                        if t == 0:
                            c, it = pairs[n]
                            pe.wait_ge(DN[l]["a_lo"], c + 2 * it + 1)
                    row_steps(steps, (a_hi, a_lo), first, last, N[2 * l + 1]["rows"],
                              last_two if last else one_step, chunk)

                down([(0, 0)], True, False)
                with pe.Fori(0, 4) as it:
                    down([(1, it)], False, False)
                    down([(2, it)], False, False)
                down([(9, 0), (10, 0)], False, True)
                if l < DEPTH - 1:
                    turn_x(2 * l + 2, 2)


def launch_arrays(x, w_qkv_ab, w_o_ab, w_qkv_c, w_o_c, ln_mix_g, ln_mix_b,
                  w_up, conv_w, conv_b, w_down, ln_ffn_g, ln_ffn_b):
    import numpy as np

    def columns(w, tiles):
        w = w.reshape(KD, P, -1, P)
        return np.stack([w[:, :, t, :].transpose(1, 0, 2).reshape(P, D) for t in tiles])

    def steps(units):
        return np.ascontiguousarray(units.reshape(-1, 2, P, UNIT).transpose(0, 2, 1, 3)).reshape(-1, P, 2 * UNIT)

    stream = []
    for l in range(DEPTH):
        order = [0, 2, 3, 4, 5, 6, 7, 1] if l == 0 else list(range(NPOS))
        w_qkv, w_o = (w_qkv_ab[0], w_o_ab[0]) if l == 0 else (w_qkv_c[0], w_o_c[0])
        q, k, v = (w_qkv[:, n * D:(n + 1) * D] for n in range(3))
        v = v.reshape(D, NPOS, P)[:, order].reshape(KD, P, D)
        o = w_o.reshape(NPOS, P, D)[order]
        if l == 0:
            q, k = (w.reshape(D, 16, 2, 32).transpose(0, 1, 3, 2).reshape(D, D) for w in (q, k))
        qk = np.stack([columns(q, order), columns(k, order)], axis=1)
        up = np.stack([columns(w_up[l], range(KF)), columns(w_up[l], range(KF, 2 * KF))], axis=1)
        for part in (qk[:1], v, qk[1:], o, up, w_down[l].reshape(KF, P, D)):
            stream.append(steps(np.ascontiguousarray(part).reshape(-1, P, UNIT)))
    taps = np.concatenate([conv_w, conv_b[:, None]], axis=1)
    taps = taps.reshape(DEPTH, 4, 2 * KF, P).transpose(3, 0, 2, 1)
    ln = np.stack([np.stack([ln_mix_g, ln_mix_b], 1), np.stack([ln_ffn_g, ln_ffn_b], 1)], 1)

    inv = np.float32(1.0) / (np.float32(10000.0) ** (np.arange(0, 64, 2, dtype=np.float32) / np.float32(64)))
    ang = (np.arange(S, dtype=np.float32)[:, None] * inv[None, :]).T
    cos, sin = np.cos(ang), np.sin(ang)
    sin = np.stack([-sin, sin], axis=1).reshape(64, S)
    rope = np.stack([np.tile(np.repeat(cos, 2, axis=0), (2, 1)), np.tile(sin, (2, 1))], axis=1)
    dist = 384 + np.arange(P)[:, None] - np.arange(S)[None, :]
    count = (dist >= 0) * ((dist <= 128) * 1 + (dist % 4 == 0) + (dist % 16 == 0))
    dilated = np.where(count > 0, -np.log(np.maximum(count, 1)), FORBID)
    masks = np.stack([dilated, np.where(dist >= 0, 0.0, FORBID)], axis=1)
    tri = np.where(np.arange(P)[None, :] < np.arange(P)[:, None], 0.0, -FORBID)
    f32 = lambda a: np.ascontiguousarray(a, dtype=np.float32)
    return {
        "x_in": x.reshape(S, D), "w_stream": np.concatenate(stream), "ident_in": f32(np.eye(P)),
        "rope_in": f32(rope), "mask_in": f32(masks), "tri_in": f32(tri),
        "conv_in": np.ascontiguousarray(taps).reshape(P, -1), "ln_in": np.ascontiguousarray(ln.reshape(2 * DEPTH, 2, D)),
    }


def kernel(**inputs):
    import numpy as np
    from concourse import bacc
    from concourse.bass_utils import run_bass_kernel_spmd

    arrays = launch_arrays(**{k: np.asarray(v) for k, v in inputs.items()})
    nc = bacc.Bacc("TRN2", target_bir_lowering=False, num_devices=1)
    args = [nc.dram_tensor(name, a.shape, F32, kind="ExternalInput").ap() for name, a in arrays.items()]
    out = nc.dram_tensor("out", (S, D), F32, kind="ExternalOutput").ap()
    build(nc, *args, out)
    r = run_bass_kernel_spmd(nc, [arrays], core_ids=[0])
    return r.results[0]["out"].reshape(1, S, D)
```
